# Optimizing a Trainium2 kernel written in Bass

```python
import jax, jax.numpy as jnp
from jax import lax
import numpy as np

D_MODEL = 1024
BATCH = 1
SEQ = 1024
DEPTH = 1

CHUNK = 64
MIX_WIDTH = D_MODEL
LRU_WIDTH = MIX_WIDTH // 2
LRU_HEADS = 8
LRU_HEAD_DIM = LRU_WIDTH // LRU_HEADS
CONV_WIDTH = 4
LRU_C = 8.0
ATTN_WIDTH = MIX_WIDTH - LRU_WIDTH
FOX_HEADS = 8
FOX_HEAD_DIM = ATTN_WIDTH // FOX_HEADS
Q_BLOCK = 128
IN_COLS = 2 * LRU_WIDTH + 3 * ATTN_WIDTH + FOX_HEADS
PEER_HEADS = 8
PEER_NKEYS = 128
PEER_N_EXPERTS = PEER_NKEYS * PEER_NKEYS
PEER_QDIM = 256
PEER_HALF = PEER_QDIM // 2
PEER_TOPK = 16
PEER_TOKEN_BLOCK = 128
RMS_EPS = 1e-6

kernel_name = 'hymba_rglru_fox_peer_block'

def rms_norm(x, g):
    xf = x.astype(jnp.float32)
    y = xf * lax.rsqrt(jnp.mean(xf * xf, axis=-1, keepdims=True) + RMS_EPS)
    return (y * g.astype(jnp.float32)).astype(x.dtype)

def causal_depthwise_conv(x, w, b):
    y = lax.conv_general_dilated(
        x, w[:, None, :].astype(x.dtype), window_strides=(1,),
        padding=[(CONV_WIDTH - 1, 0)],
        dimension_numbers=('NWC', 'WIO', 'NWC'),
        feature_group_count=x.shape[-1])
    return y + b.astype(x.dtype)

def rg_lru(x, w_a, b_a, w_x, b_x, lam):
    bsz, s, _ = x.shape
    xf = x.astype(jnp.float32)
    xh = xf.reshape(bsz, s, LRU_HEADS, LRU_HEAD_DIM)
    r = jax.nn.sigmoid(jnp.einsum('bshi,hij->bshj', xh, w_a.astype(jnp.float32)).reshape(bsz, s, LRU_WIDTH) + b_a.astype(jnp.float32))
    i = jax.nn.sigmoid(jnp.einsum('bshi,hij->bshj', xh, w_x.astype(jnp.float32)).reshape(bsz, s, LRU_WIDTH) + b_x.astype(jnp.float32))
    log_a = -LRU_C * r * jax.nn.softplus(-lam.astype(jnp.float32))
    a = jnp.exp(log_a)
    u = jnp.sqrt(-jnp.expm1(2.0 * log_a)) * (i * xf)

    def combine(left, right):
        a1, b1 = left
        a2, b2 = right
        return a1 * a2, a2 * b1 + b2

    _, h = lax.associative_scan(combine, (a, u), axis=1)
    return h

def forgetting_attention(q, k, v, log_f):
    bsz, s, nh, dh = q.shape
    F = jnp.cumsum(log_f.astype(jnp.float32), axis=1).transpose(0, 2, 1)
    qh = q.astype(jnp.float32).transpose(0, 2, 1, 3) * (dh ** -0.5)
    kh = k.astype(jnp.float32).transpose(0, 2, 1, 3)
    vh = v.astype(jnp.float32).transpose(0, 2, 1, 3)
    kpos = jnp.arange(s)

    def block(bi):
        start = bi * Q_BLOCK
        qb = lax.dynamic_slice_in_dim(qh, start, Q_BLOCK, axis=2)
        fq = lax.dynamic_slice_in_dim(F, start, Q_BLOCK, axis=2)
        qpos = start + jnp.arange(Q_BLOCK)
        logits = jnp.einsum('bhqd,bhkd->bhqk', qb, kh) + fq[..., :, None] - F[..., None, :]
        logits = jnp.where(kpos[None, :] <= qpos[:, None], logits, -jnp.inf)
        p = jax.nn.softmax(logits, axis=-1)
        return jnp.einsum('bhqk,bhkd->bhqd', p, vh)

    out = lax.map(block, jnp.arange(s // Q_BLOCK))
    return out.transpose(1, 0, 3, 2, 4).reshape(bsz, s, nh * dh)

def peer(h, w_q, subkeys, u_tab, v_tab):
    bsz, s, d = h.shape
    t = bsz * s
    hf = h.reshape(t, d)
    q = (hf @ w_q).astype(jnp.float32).reshape(t, PEER_HEADS, 2, PEER_HALF)
    sc = jnp.einsum('thpc,hpnc->thpn', q, subkeys.astype(jnp.float32))
    s1, i1 = lax.top_k(sc[:, :, 0], PEER_TOPK)
    s2, i2 = lax.top_k(sc[:, :, 1], PEER_TOPK)
    cand = (s1[..., :, None] + s2[..., None, :]).reshape(t, PEER_HEADS, PEER_TOPK * PEER_TOPK)
    top_s, top_p = lax.top_k(cand, PEER_TOPK)
    e1 = jnp.take_along_axis(i1, top_p // PEER_TOPK, axis=-1)
    e2 = jnp.take_along_axis(i2, top_p % PEER_TOPK, axis=-1)
    hk = PEER_HEADS * PEER_TOPK
    experts = (e1 * PEER_NKEYS + e2).reshape(t, hk)
    gates = jax.nn.softmax(top_s, axis=-1).reshape(t, hk)
    nb = t // PEER_TOKEN_BLOCK

    def block(args):
        xb, eb, gb = args
        pre = jnp.einsum('td,tkd->tk', xb.astype(jnp.float32), u_tab[eb].astype(jnp.float32))
        act = jax.nn.gelu(pre) * gb
        return jnp.einsum('tk,tkd->td', act, v_tab[eb].astype(jnp.float32))

    y = lax.map(block, (hf.reshape(nb, PEER_TOKEN_BLOCK, d),
                        experts.reshape(nb, PEER_TOKEN_BLOCK, hk),
                        gates.reshape(nb, PEER_TOKEN_BLOCK, hk)))
    return y.reshape(bsz, s, d).astype(h.dtype)

def setup_inputs(seed: int = 0) -> dict:
    key = jax.random.key(seed)
    ks = jax.random.split(key, 24)
    f32 = jnp.float32

    def nrm(k, shape, scale):
        return jax.random.normal(k, shape, f32) * scale

    a0 = jax.random.uniform(ks[9], (DEPTH, LRU_WIDTH), f32, 0.9, 0.999)
    return {
        'x': nrm(ks[0], (BATCH, SEQ, D_MODEL), 1.0),
        'norm1_g': 1.0 + nrm(ks[1], (DEPTH, D_MODEL), 0.01),
        'w_in': nrm(ks[2], (DEPTH, D_MODEL, IN_COLS), D_MODEL ** -0.5),
        'conv_w': nrm(ks[3], (DEPTH, CONV_WIDTH, LRU_WIDTH), CONV_WIDTH ** -0.5),
        'conv_b': nrm(ks[4], (DEPTH, LRU_WIDTH), 0.01),
        'lru_wa': nrm(ks[5], (DEPTH, LRU_HEADS, LRU_HEAD_DIM, LRU_HEAD_DIM), LRU_HEAD_DIM ** -0.5),
        'lru_ba': nrm(ks[6], (DEPTH, LRU_WIDTH), 0.01),
        'lru_wx': nrm(ks[7], (DEPTH, LRU_HEADS, LRU_HEAD_DIM, LRU_HEAD_DIM), LRU_HEAD_DIM ** -0.5),
        'lru_bx': nrm(ks[8], (DEPTH, LRU_WIDTH), 0.01),
        'lru_lambda': jnp.log(a0) - jnp.log1p(-a0),
        'fox_bf': jax.random.uniform(ks[10], (DEPTH, FOX_HEADS), f32, 1.0, 4.0),
        'gn_lru_g': 1.0 + nrm(ks[11], (DEPTH, LRU_WIDTH), 0.01),
        'gn_fox_g': 1.0 + nrm(ks[12], (DEPTH, ATTN_WIDTH), 0.01),
        'w_out': nrm(ks[13], (DEPTH, MIX_WIDTH, D_MODEL), MIX_WIDTH ** -0.5),
        'norm2_g': 1.0 + nrm(ks[14], (DEPTH, D_MODEL), 0.01),
        'peer_wq': nrm(ks[15], (DEPTH, D_MODEL, PEER_HEADS * PEER_QDIM), D_MODEL ** -0.5),
        'peer_subkeys': nrm(ks[16], (DEPTH, PEER_HEADS, 2, PEER_NKEYS, PEER_HALF), PEER_HALF ** -0.5),
        'peer_u': nrm(ks[17], (DEPTH, PEER_N_EXPERTS, D_MODEL), D_MODEL ** -0.5),
        'peer_v': nrm(ks[18], (DEPTH, PEER_N_EXPERTS, D_MODEL), 0.25),
        'final_g': 1.0 + nrm(ks[19], (D_MODEL,), 0.01),
    }

def reference(x, norm1_g, w_in, conv_w, conv_b, lru_wa, lru_ba, lru_wx, lru_bx,
              lru_lambda, fox_bf, gn_lru_g, gn_fox_g, w_out, norm2_g, peer_wq,
              peer_subkeys, peer_u, peer_v, final_g):
    bsz, s, _ = x.shape
    cuts = [LRU_WIDTH, 2 * LRU_WIDTH, 2 * LRU_WIDTH + ATTN_WIDTH,
            2 * LRU_WIDTH + 2 * ATTN_WIDTH, 2 * LRU_WIDTH + 3 * ATTN_WIDTH]
    for l in range(DEPTH):
        h = rms_norm(x, norm1_g[l])
        proj = h @ w_in[l]
        xr, gr, q, k, v, fl = jnp.split(proj, cuts, axis=-1)
        xr = causal_depthwise_conv(xr, conv_w[l], conv_b[l])
        y_lru = rg_lru(xr, lru_wa[l], lru_ba[l], lru_wx[l], lru_bx[l], lru_lambda[l])
        y_lru = y_lru * jax.nn.gelu(gr.astype(jnp.float32))
        log_f = jax.nn.log_sigmoid(fl.astype(jnp.float32) + fox_bf[l].astype(jnp.float32))
        y_fox = forgetting_attention(
            q.reshape(bsz, s, FOX_HEADS, FOX_HEAD_DIM),
            k.reshape(bsz, s, FOX_HEADS, FOX_HEAD_DIM),
            v.reshape(bsz, s, FOX_HEADS, FOX_HEAD_DIM), log_f)
        y_mix = jnp.concatenate([rms_norm(y_lru, gn_lru_g[l]),
                                 rms_norm(y_fox, gn_fox_g[l])], axis=-1).astype(x.dtype)
        x = x + y_mix @ w_out[l]
        h2 = rms_norm(x, norm2_g[l])
        x = x + peer(h2, peer_wq[l], peer_subkeys[l], peer_u[l], peer_v[l])
    return rms_norm(x, final_g)


_drawn_inputs = setup_inputs


def setup_inputs(seed=0):
    import zlib

    import numpy as np

    out = dict(_drawn_inputs(seed))
    spreads = {}
    factors = {'norm1_g': 3.656,
     'lru_ba': 33.072,
     'lru_bx': 31.805,
     'gn_lru_g': 40.191,
     'gn_fox_g': 41.646,
     'norm2_g': 37.623,
     'final_g': 32.132,
     'conv_b': 7.257}
    for name, (base, spread) in spreads.items():
        noise = np.random.default_rng([zlib.crc32(name.encode()), seed]).standard_normal(out[name].shape)
        drawn = base * np.exp(spread * noise) if base else spread * noise
        out[name] = __import__('jax').numpy.asarray(drawn.astype(out[name].dtype))
    for name, factor in factors.items():
        out[name] = (out[name] * factor).astype(out[name].dtype)
    return out
```

```python
from contextlib import ExitStack
import concourse.bass as bass
from concourse import mybir

ALU = mybir.AluOpType
ACT = mybir.ActivationFunctionType
AX_X = mybir.AxisListType.X
F32 = mybir.dt.float32
F32R = mybir.dt.float32r
U32 = mybir.dt.uint32
I32 = mybir.dt.int32

P = 128
HALF = 512
EPS = 1e-6
LRU_C = 8.0
BIG = 1e30
LOWEST = -3.0e38
LOG1P_TERMS = 8


class Parts:
    pass


class Done:

    def __init__(self, engine, semaphore):
        self.engine, self.semaphore, self.count, self.base = engine, semaphore, 0, 0

    def mark(self, instruction):
        instruction.then_inc(self.semaphore, 1)
        self.count += 1
        return self.count

    def wait(self, count):
        self.engine.wait_ge(self.semaphore, self.base + count)

    def link(self, instruction):
        self.wait(self.mark(instruction))

    def link_apart(self, instruction, count_waits):
        self.link(instruction)
        self.engine.sem_inc(count_waits, 1)

    def enter(self, i, per_pass):
        self.count, self.base = 0, i * per_pass


def halves(n=2):
    return [slice(h * HALF, (h + 1) * HALF) for h in range(n)]


def log1p_series(dve, own, e, s, s2, acc):
    own.link(dve.tensor_scalar(s, e, 2.0, None, ALU.add))
    own.link(dve.reciprocal(s, s))
    own.link(dve.tensor_tensor(s, s, e, ALU.mult))
    own.link(dve.tensor_tensor(s2, s, s, ALU.mult))
    own.link(dve.tensor_scalar(acc, s2, 1.0 / (2 * LOG1P_TERMS - 1), None, ALU.mult))
    for n in range(LOG1P_TERMS - 2, 0, -1):
        own.link(dve.scalar_tensor_tensor(out=acc, in0=acc, scalar=1.0 / (2 * n + 1), in1=s2,
                                          op0=ALU.add, op1=ALU.mult))
    own.link(dve.tensor_scalar(acc, acc, 1.0, 2.0, ALU.add, ALU.mult))
    own.link(dve.tensor_tensor(acc, acc, s, ALU.mult))


def project(nc, d, m, sem):
    D, S, G = d.D, d.S, d.GROUP
    KT, NT, CT = D // P, S // P, G // P
    GROUPS = 5
    with ExitStack() as own_memory:
        sb = lambda n, s, t=F32: own_memory.enter_context(nc.sbuf_tensor(n, s, t))
        ps = lambda n, s: own_memory.enter_context(nc.psum_tensor(n, s, F32))
        x_rows = sb("x_rows", [P, NT, D])
        gain = sb("gain1", [P, D])
        h_rows = sb("h_rows", [P, 2, D])
        hT = sb("hT", [P, KT, S])
        w = sb("w_in_group", [P, 2, KT, G])
        wf = sb("w_forget", [P, KT, d.FH])
        squares = sb("squares1", [P, D])
        sums = sb("sums1", [P, NT])
        rstd = sb("rstd1", [P, NT])
        fbias = sb("forget_bias", [d.FH, 1])
        turned = ps("turned1", [P, 2, KT, P])
        product = ps("product1", [P, 4, HALF])

        x_in = [sem(f"x_in{b}") for b in range(NT)]
        small_in, gain_in = sem("small1_in"), sem("gain1_in")
        w_in = [sem("w_in0"), sem("w_in1")]
        summed, rooted, dve1 = sem("x_summed"), sem("x_rooted"), sem("dve1")
        turned_done, turned_read = sem("h_turned"), sem("h_turned_read")
        product_done, product_read = sem("product_done"), sem("product_read")

        with nc.Block() as block:
            @block.sync
            def _(sp):
                for b in range(NT):
                    sp.dma_start(x_rows[:, b, :], d.x[b * P:(b + 1) * P, :]).then_inc(x_in[b], 16)
                    if b == 0:
                        sp.dma_start(gain[:], d.norm1_g.partition_broadcast(P)).then_inc(gain_in, 16)
                for g in range(GROUPS):
                    if g >= 2:
                        sp.wait_ge(product_read, (g - 1) * 2 * CT)
                    sp.dma_start(w[:, g % 2], d.w_in[:, g * G:(g + 1) * G].rearrange("(k p) n -> p k n", p=P)
                                 ).then_inc(w_in[g % 2], 16)

            @block.gpsimd
            def _(pool):
                pool.dma_start(wf[:], d.w_in[:, GROUPS * G:].rearrange("(k p) n -> p k n", p=P)).then_inc(small_in, 16)
                pool.wait_ge(small_in, 16)
                pool.dma_start(fbias[:], d.fox_bf.rearrange("(a b) -> a b", b=1)).then_inc(small_in, 16)

            @block.scalar
            def _(act):
                for b in range(NT):
                    act.wait_ge(x_in[b], 16)
                    if b:
                        act.wait_ge(summed, b)
                    nc.scalar.activation(squares[:], x_rows[:, b, :], ACT.Square,
                                         accum_out=sums[:, b:b + 1]).then_inc(summed, 1)
                act.wait_ge(dve1, 2)
                nc.scalar.activation(sums[:], sums[:], ACT.Sqrt).then_inc(rooted, 1)
                for b in range(NT):
                    act.wait_ge(turned_done, b + 1)
                    nc.scalar.activation(hT[:, :, b * P:(b + 1) * P], turned[:, b % 2], ACT.Copy
                                         ).then_inc(turned_read, 1)

                n = 0
                for g, (to, func, scale) in enumerate([(m.xrT, ACT.Copy, 1.0), (m.gateT, ACT.Gelu_apprx_tanh, 1.0),
                                                       (m.qT, ACT.Copy, -d.QSCALE), (m.kT, ACT.Copy, 1.0)]):
                    pad = d.PAD if g == 0 else 0
                    for c in range(CT):
                        for cols in halves(S // HALF):
                            act.wait_ge(product_done, n + 1)
                            nc.scalar.activation(to[:, c, pad + cols.start:pad + cols.stop], product[:, n % 4],
                                                 func, scale=scale).then_inc(product_read, 1)
                            n += 1
                for b in range(NT):
                    act.wait_ge(product_done, n + 1)
                    nc.scalar.activation(m.v[:, b, :], product[:, n % 4], ACT.Copy).then_inc(product_read, 1)
                    n += 1
                act.wait_ge(small_in, 32)
                for cols in halves(S // HALF):
                    act.wait_ge(product_done, n + 1)
                    nc.scalar.activation(m.forget[:, cols], product[0:d.FH, n % 4], ACT.Identity,
                                         bias=fbias[:]).then_inc(product_read, 1)
                    n += 1

            @block.vector
            def _(dve):
                v = nc.vector
                own = Done(dve, dve1)
                own.mark(v.memset(m.xrT[:, :, 0:d.PAD], 0.0))
                dve.wait_ge(summed, NT)
                own.link(v.tensor_scalar(sums[:], sums[:], 1.0 / D, EPS, ALU.mult, ALU.add))
                dve.wait_ge(rooted, 1)
                own.link(v.reciprocal(rstd[:], sums[:]))
                dve.wait_ge(gain_in, 16)
                for b in range(NT):
                    if b >= 2:
                        dve.wait_ge(turned_done, b - 1)
                    own.mark(v.scalar_tensor_tensor(out=h_rows[:, b % 2], in0=x_rows[:, b, :], scalar=rstd[:, b:b + 1],
                                                    in1=gain[:], op0=ALU.mult, op1=ALU.mult))

            @block.tensor
            def _(pe):
                pe.wait_ge(m.ident_ready, 2)
                for b in range(NT):
                    pe.wait_ge(dve1, 4 + b)
                    if b >= 2:
                        pe.wait_ge(turned_read, b - 1)
                    for k in range(KT):
                        last = nc.tensor.transpose(turned[:, b % 2, k], h_rows[:, b % 2, k * P:(k + 1) * P], m.ident[:])
                    last.then_inc(turned_done, 1)
                pe.wait_ge(turned_read, NT)
                n = 0

                def product_bank():
                    if n >= 4:
                        pe.wait_ge(product_read, n - 3)

                for g in range(4):
                    pe.wait_ge(w_in[g % 2], 16 * (g // 2 + 1))
                    for c in range(CT):
                        for cols in halves(S // HALF):
                            product_bank()
                            for k in range(KT):
                                last = nc.tensor.matmul(product[:, n % 4], w[:, g % 2, k, c * P:(c + 1) * P],
                                                        hT[:, k, cols], start=k == 0, stop=k == KT - 1)
                            last.then_inc(product_done, 1)
                            n += 1
                pe.wait_ge(w_in[0], 16 * 3)
                for b in range(NT):
                    product_bank()
                    for k in range(KT):
                        last = nc.tensor.matmul(product[:, n % 4], hT[:, k, b * P:(b + 1) * P], w[:, 0, k],
                                                start=k == 0, stop=k == KT - 1)
                    last.then_inc(product_done, 1)
                    n += 1
                pe.wait_ge(small_in, 32)
                for cols in halves(S // HALF):
                    product_bank()
                    for k in range(KT):
                        last = nc.tensor.matmul(product[0:d.FH, n % 4], wf[:, k, :], hT[:, k, cols],
                                                start=k == 0, stop=k == KT - 1)
                    last.then_inc(product_done, 1)
                    n += 1


def recur(nc, d, m, sem):
    S, CT = d.S, d.GROUP // P
    HD = d.LHD
    with ExitStack() as own_memory:
        sb = lambda n, s, t=F32: own_memory.enter_context(nc.sbuf_tensor(n, s, t))
        ps = lambda n, s: own_memory.enter_context(nc.psum_tensor(n, s, F32))
        wa = sb("wa_blocks", [P, CT, P])
        wx = sb("wx_blocks", [P, CT, P])
        taps = sb("conv_taps", [P, CT, d.TAPS])
        vec = sb("lru_vectors", [P, 5, CT])
        xc = sb("x_conv", [P, CT, S])
        r = sb("r_gate", [P, CT, S])
        ig = sb("i_gate", [P, CT, S])
        tanh = sb("tanh_m", [P, CT, S])
        tmp = sb("lru_tmp", [P, S])
        sp_e, sp_s, sp_q, sp_a = (sb(f"softplus_{n}", [P, CT]) for n in "esqa")
        decay = sb("decay", [P, CT])
        ndecay = sb("minus_decay", [P, CT])
        fe, fs, fq, fa = (sb(f"forget_{n}", [d.FH, S]) for n in "esqa")
        ones = sb("ones_row", [d.FH, S])
        gates = ps("gates", [P, 3, 2, HALF])
        ssq = ps("ssq_lru", [P, HALF])

        vec_in, taps_in, blocks_in = sem("vec_in"), sem("taps_in"), sem("blocks_in")
        dve2, act2, pe2 = sem("dve2"), sem("act2"), sem("pe2")
        zeroed = sem("blocks_zeroed")

        with nc.Block() as block:
            @block.gpsimd
            def _(pool):
                pool.memset(wa[:], 0.0).then_inc(zeroed, 1)
                pool.memset(wx[:], 0.0).then_inc(zeroed, 1)

            @block.sync
            def _(sp):
                for n, a in enumerate([d.conv_b, d.lru_ba, d.lru_bx, d.lru_lambda, d.gn_lru_g]):
                    if n:
                        sp.wait_ge(vec_in, 16 * n)
                    sp.dma_start(vec[:, n], a.rearrange("(c p) -> p c", p=P),
                                 allow_slow_non_contiguous=True).then_inc(vec_in, 16)
                for j in range(d.TAPS):
                    if j:
                        sp.wait_ge(taps_in, 16 * j)
                    sp.dma_start(taps[:, :, j], d.conv_w[j].rearrange("(c p) -> p c", p=P),
                                 allow_slow_non_contiguous=True).then_inc(taps_in, 16)
                sp.wait_ge(zeroed, 2)
                n = 0
                for to, src in ((wa, d.lru_wa), (wx, d.lru_wx)):
                    for o in range(P // HD):
                        part = slice(o * HD, (o + 1) * HD)
                        if n:
                            sp.wait_ge(blocks_in, 16 * n)
                        sp.dma_start(to[part, :, part], src.rearrange("(c o) i j -> o i c j", o=P // HD)[o]
                                     ).then_inc(blocks_in, 16)
                        n += 1

            @block.tensor
            def _(pe):
                pe.wait_ge(blocks_in, 64)
                n = 0
                for c in range(CT):
                    pe.wait_ge(dve2, d.TAPS * (c + 1))
                    for w in (wa, wx):
                        if n >= 3:
                            pe.wait_ge(act2, n - 2)
                        for half, cols in enumerate(halves(2)):
                            last = nc.tensor.matmul(gates[:, n % 3, half], w[:, c, :], xc[:, c, cols],
                                                    start=True, stop=True)
                        last.then_inc(pe2, 1)
                        n += 1
                pe.wait_ge(act2, 2 * CT + 2 + 2 * CT + CT + CT)
                for b in range(S // P):
                    for c in range(CT):
                        last = nc.tensor.matmul(ssq[:, b:b + 1], r[:, c, b * P:(b + 1) * P], m.ones_col[:],
                                                start=c == 0, stop=c == CT - 1)
                last.then_inc(pe2, 1)

            @block.vector
            def _(dve):
                v = nc.vector
                own = Done(dve, dve2)
                dve.wait_ge(vec_in, 80)
                dve.wait_ge(taps_in, 16 * d.TAPS)
                for c in range(CT):
                    own.link(v.tensor_scalar(xc[:, c, :], m.xrT[:, c, 0:S], taps[:, c, 0:1], vec[:, 0, c:c + 1],
                                             ALU.mult, ALU.add))
                    for j in range(1, d.TAPS):
                        own.link(v.scalar_tensor_tensor(out=xc[:, c, :], in0=m.xrT[:, c, j:j + S],
                                                        scalar=taps[:, c, j:j + 1], in1=xc[:, c, :],
                                                        op0=ALU.mult, op1=ALU.add))
                dve.wait_ge(act2, 2 * CT + 2)
                log1p_series(v, own, sp_e[:], sp_s[:], sp_q[:], sp_a[:])
                own.link(v.tensor_scalar(sp_s[:], vec[:, 3], -1.0, 0.0, ALU.mult, ALU.max))
                own.link(v.tensor_tensor(sp_a[:], sp_a[:], sp_s[:], ALU.add))
                own.link(v.tensor_scalar(decay[:], sp_a[:], LRU_C, None, ALU.mult))
                own.link(v.tensor_scalar(ndecay[:], sp_a[:], -LRU_C, None, ALU.mult))
                d.SOFTPLUS_DONE = own.count
                for c in range(CT):
                    dve.wait_ge(act2, 2 * CT + 2 + 2 * c + 1)
                    own.link(v.tensor_scalar(tmp[:], tanh[:, c, :], 1.0, None, ALU.add))
                    own.link(v.reciprocal(tmp[:], tmp[:]))
                    own.link(v.scalar_tensor_tensor(out=tanh[:, c, :], in0=tanh[:, c, :], scalar=2.0, in1=tmp[:],
                                                    op0=ALU.mult, op1=ALU.mult))
                d.SCAN_DONE = own.count
                for c in range(CT):
                    dve.wait_ge(act2, 2 * CT + 2 + 2 * CT + c + 1)
                    own.link(v.tensor_tensor(xc[:, c, :], xc[:, c, :], ig[:, c, :], ALU.mult))
                    own.link(v.tensor_tensor(xc[:, c, :], xc[:, c, :], tanh[:, c, :], ALU.mult))
                    own.link(v.tensor_tensor_scan(out=ig[:, c, :], data0=r[:, c, :], data1=xc[:, c, :], initial=0.0,
                                                  op0=ALU.mult, op1=ALU.add))
                    own.link(v.tensor_tensor(m.gateT[:, c, :], m.gateT[:, c, :], ig[:, c, :], ALU.mult))
                for c in range(CT):
                    dve.wait_ge(act2, 2 * CT + 2 + 3 * CT + c + 1)
                    own.link(v.tensor_scalar(m.gateT[:, c, :], m.gateT[:, c, :], vec[:, 4, c:c + 1], None, ALU.mult))
                dve.wait_ge(act2, 2 * CT + 2 + 4 * CT + 2)
                log1p_series(v, own, fe[:], fs[:], fq[:], fa[:])
                own.link(v.tensor_scalar(fs[:], m.forget[:], 0.0, None, ALU.min))
                own.link(v.tensor_tensor(fs[:], fs[:], fa[:], ALU.subtract))
                own.link(v.memset(ones[:], 1.0))
                own.link(v.tensor_tensor_scan(out=m.forget[:], data0=ones[:], data1=fs[:], initial=0.0,
                                              op0=ALU.mult, op1=ALU.add))
                dve.wait_ge(pe2, 2 * CT + 1)
                own.link(v.tensor_scalar(m.rstd_lru[:], ssq[:, 0:S // P], 1.0 / d.GROUP, EPS, ALU.mult, ALU.add))

            @block.scalar
            def _(act):
                own = Done(act, act2)
                A = nc.scalar.activation
                act.wait_ge(vec_in, 80)
                n = 0
                for c in range(CT):
                    for to, bias in ((r, 1), (ig, 2)):
                        act.wait_ge(pe2, n + 1)
                        own.mark(A(to[:, c, :], gates[:, n % 3].rearrange("p a b -> p (a b)"), ACT.Sigmoid,
                                   bias=vec[:, bias, c:c + 1]))
                        n += 1
                own.link(A(sp_e[:], vec[:, 3], ACT.Abs))
                own.link(A(sp_e[:], sp_e[:], ACT.Exp, scale=-1.0))
                for c in range(CT):
                    if c == 0:
                        act.wait_ge(dve2, d.SOFTPLUS_DONE)
                    own.mark(A(tanh[:, c, :], r[:, c, :], ACT.Tanh, scale=decay[:, c:c + 1]))
                    own.wait(own.count)
                    own.mark(A(r[:, c, :], r[:, c, :], ACT.Exp, scale=ndecay[:, c:c + 1]))
                for c in range(CT):
                    act.wait_ge(dve2, d.SOFTPLUS_DONE + 3 * (c + 1))
                    own.mark(A(tanh[:, c, :], tanh[:, c, :], ACT.Sqrt))
                for c in range(CT):
                    act.wait_ge(dve2, d.SCAN_DONE + 4 * c + 4)
                    own.mark(A(r[:, c, :], m.gateT[:, c, :], ACT.Square))
                own.link(A(fe[:], m.forget[:], ACT.Abs))
                own.link(A(fe[:], fe[:], ACT.Exp, scale=-1.0))


def attend(nc, d, m, sem):
    S, NT, HD, FH = d.S, d.S // P, d.FHD, d.FH
    PAIRS = FH // 2
    ITEMS = 2 * NT
    with ExitStack() as own_memory:
        sb = lambda n, s, t=F32: own_memory.enter_context(nc.sbuf_tensor(n, s, t))
        ps = lambda n, s: own_memory.enter_context(nc.psum_tensor(n, s, F32))
        pick = sb("pick_head", [FH, FH, P])
        later = sb("later_keys", [P, P])
        Fb = sb("forget_sums", [P, FH, S])
        Fp = sb("forget_sums_pair", [P, 2, S])
        Fm = sb("forget_sums_masked", [P, 2, S])
        qp, kp = sb("q_pair", [P, S]), sb("k_pair", [P, S])
        vp = sb("v_pair", [P, NT, P])
        neg = sb("neg_logits", [P, 2, S])
        low = sb("lowest", [P, 2, 2])
        prob = sb("probs", [P, 2, S])
        total = sb("totals", [P, 2])
        inv = sb("inv_totals", [P, 2])
        probT = sb("probs_turned", [P, 2, S])
        logit = ps("logits", [P, 2, 2, HALF])
        turned = ps("probs_turned_ps", [P, 2, 4, P])
        mixed = ps("mixed_values", [P, 2, HALF])

        low_done, act3, pool3 = sem("low_done"), sem("sums_spread"), sem("pair_copied")
        logits_done, logits_read = sem("logits_done"), sem("logits_read")
        probs_done = sem("probs_done")
        part_turned, part_read = sem("part_turned"), sem("part_read")
        mixed_done, mixed_read = sem("mixed_done"), sem("mixed_read")
        inv_done, picked = sem("inv_done"), sem("picked")
        fb_done, fp_done, fm_done = sem("fb_done"), sem("fp_done"), sem("fm_done")
        pool_apart = sem("attend_pool_waits")
        apart = sem("attend_waits")
        PARTS = sum((qt + 4) // 4 for qt in range(NT)) * 2

        with nc.Block() as block:
            @block.gpsimd
            def _(pool):
                pool.memset(pick[:], 0.0).then_inc(picked, 1)
                pool.wait_ge(picked, 1)
                pool.affine_select(out=pick[:], in_=pick[:], compare_op=ALU.not_equal, fill=1.0, base=0,
                                   pattern=[[-1, FH], [0, P]], channel_multiplier=1).then_inc(picked, 1)
                pool.memset(later[:], 0.0).then_inc(picked, 1)
                pool.wait_ge(picked, 3)
                pool.affine_select(out=later[:], in_=later[:], compare_op=ALU.is_ge, fill=BIG, base=0,
                                   pattern=[[-1, P]], channel_multiplier=1).then_inc(picked, 1)
                with pool.Fori(0, PAIRS) as i:
                    pool.wait_ge(mixed_done, i * ITEMS + 1)
                    pool.sem_inc(pool_apart, 1)
                    pool.tensor_copy(qp[:], m.qT[:, bass.ds(i, 1), :].rearrange("p a s -> p (a s)")).then_inc(pool3, 1)
                    pool.tensor_copy(kp[:], m.kT[:, bass.ds(i, 1), :].rearrange("p a s -> p (a s)")).then_inc(pool3, 1)
                    pool.tensor_copy(vp[:], m.v[:, :, bass.ds(i * P, P)]).then_inc(pool3, 1)

            @block.tensor
            def _(pe):
                pe.wait_ge(picked, 4)
                pe.sem_inc(mixed_done, 1)
                for h in range(FH):
                    if h >= 2:
                        pe.wait_ge(act3, h - 1)
                    for half, cols in enumerate(halves(2)):
                        last = nc.tensor.matmul(logit[:, h % 2, half], pick[:, h, :], m.forget[:, cols],
                                                start=True, stop=True)
                    last.then_inc(fb_done, 1)
                pe.wait_ge(act3, FH)

                def scores(i, n):
                    h, qt = divmod(n, NT)
                    part = slice(h * HD, (h + 1) * HD)
                    pe.wait_ge(logits_read, i * ITEMS + n + 1)
                    for half in range(qt // 4 + 1):
                        width = min(HALF, (qt + 1) * P - half * HALF)
                        last = nc.tensor.matmul(logit[:, n % 2, half, 0:width], qp[part, qt * P:(qt + 1) * P],
                                                kp[part, half * HALF:half * HALF + width], start=True, stop=True)
                    last.then_inc(logits_done, 1)

                with pe.Fori(0, PAIRS) as i:
                    pe.wait_ge(pool3, (i + 1) * 3)
                    scores(i, 0)
                    part_no = 0
                    for n in range(ITEMS):
                        h, qt = divmod(n, NT)
                        if n + 1 < ITEMS:
                            scores(i, n + 1)
                        pe.wait_ge(probs_done, i * ITEMS + n + 1)
                        for g in range(0, qt + 1, 4):
                            pe.wait_ge(part_read, i * PARTS + part_no + 1)
                            for kb in range(g, min(g + 4, qt + 1)):
                                last = nc.tensor.transpose(turned[:, part_no % 2, kb - g],
                                                           prob[:, n % 2, kb * P:(kb + 1) * P], m.ident[:])
                            last.then_inc(part_turned, 1)
                            part_no += 1
                        pe.wait_ge(part_read, i * PARTS + part_no + 2)
                        pe.wait_ge(mixed_read, i * ITEMS + n + 1)
                        for kb in range(qt + 1):
                            last = nc.tensor.matmul(mixed[:, n % 2, 0:HD], probT[:, n % 2, kb * P:(kb + 1) * P],
                                                    vp[:, kb, h * HD:(h + 1) * HD], start=kb == 0, stop=kb == qt)
                        last.then_inc(mixed_done, 1)
                    assert part_no == PARTS

            @block.scalar
            def _(act):
                act.sem_inc(part_read, 2)
                for h in range(FH):
                    act.wait_ge(fb_done, h + 1)
                    nc.scalar.activation(Fb[:, h, :], logit[:, h % 2].rearrange("p a b -> p (a b)"), ACT.Copy
                                         ).then_inc(act3, 1)
                act.wait_ge(act3, FH)
                with act.Fori(0, PAIRS) as i:
                    act.wait_ge(logits_read, i * ITEMS + 2)
                    nc.scalar.activation(Fp[:], Fb[:, bass.ds(2 * i, 2), :], ACT.Copy).then_inc(fp_done, 1)
                    part_no = 0
                    for n in range(ITEMS):
                        qt = n % NT
                        W = (qt + 1) * P
                        act.wait_ge(logits_read, i * ITEMS + n + 3)
                        nc.scalar.activation(prob[:, n % 2, 0:W], neg[:, n % 2, 0:W], ACT.Exp, scale=-1.0,
                                             bias=low[:, n % 2, 1:2], accum_out=total[:, n % 2:n % 2 + 1]
                                             ).then_inc(probs_done, 1)
                        if n:
                            act.wait_ge(mixed_done, i * ITEMS + n)
                        for g in range(0, qt + 1, 4):
                            k = min(4, qt + 1 - g)
                            act.wait_ge(part_turned, i * PARTS + part_no + 1)
                            nc.scalar.activation(probT[:, n % 2, g * P:(g + k) * P],
                                                 turned[:, part_no % 2, 0:k].rearrange("p a b -> p (a b)"),
                                                 ACT.Copy).then_inc(part_read, 1)
                            part_no += 1

            @block.vector
            def _(dve):
                v = nc.vector
                dve.sem_inc(logits_read, 2)
                dve.sem_inc(mixed_read, 2)
                with dve.Fori(0, PAIRS) as i:
                    dve.wait_ge(fp_done, i + 1)
                    v.tensor_tensor(Fm[:].rearrange("p h (a b) -> p (h a) b", b=P),
                                    Fp[:].rearrange("p h (a b) -> p (h a) b", b=P),
                                    later[:].rearrange("p (a b) -> p a b", a=1).to_broadcast([P, 2 * NT, P]),
                                    ALU.add).then_inc(fm_done, 1)
                    dve.wait_ge(fm_done, i + 1)

                    def finish(n):
                        h, qt = divmod(n, NT)
                        dve.wait_ge(probs_done, i * ITEMS + n + 1)
                        v.reciprocal(inv[:, n % 2:n % 2 + 1], total[:, n % 2:n % 2 + 1]).then_inc(inv_done, 1)
                        dve.wait_ge(inv_done, i * ITEMS + n + 1)
                        dve.wait_ge(mixed_done, i * ITEMS + n + 2)
                        v.tensor_scalar(m.fox[:, qt, bass.ds(i * P + h * HD, HD)], mixed[:, n % 2, 0:HD],
                                        inv[:, n % 2:n % 2 + 1], None, ALU.mult).then_inc(mixed_read, 1)

                    for n in range(ITEMS):
                        h, qt = divmod(n, NT)
                        dve.wait_ge(logits_done, i * ITEMS + n + 1)
                        if n >= 2:
                            dve.wait_ge(probs_done, i * ITEMS + n - 1)
                        dve.sem_inc(apart, 1)
                        src = logit[:, n % 2].rearrange("p a b -> p (a b)")
                        if qt:
                            v.tensor_tensor_reduce(out=neg[:, n % 2, 0:qt * P], in0=src[:, 0:qt * P],
                                                   in1=Fp[:, h, 0:qt * P], scale=1.0, scalar=3.0e38, op0=ALU.add,
                                                   op1=ALU.min, accum_out=low[:, n % 2, 0:1]).then_inc(low_done, 1)
                        else:
                            v.memset(low[:, n % 2, 0:1], 3.0e38).then_inc(low_done, 1)
                        dve.wait_ge(low_done, i * ITEMS + n + 1)
                        dve.sem_inc(apart, 1)
                        v.tensor_tensor_reduce(out=neg[:, n % 2, qt * P:(qt + 1) * P], in0=src[:, qt * P:(qt + 1) * P],
                                               in1=Fm[:, h, qt * P:(qt + 1) * P], scale=1.0,
                                               scalar=low[:, n % 2, 0:1], op0=ALU.add, op1=ALU.min,
                                               accum_out=low[:, n % 2, 1:2]).then_inc(logits_read, 1)
                        if n:
                            finish(n - 1)
                    finish(ITEMS - 1)


def mix_out(nc, d, m, sem):
    D, S, G = d.D, d.S, d.GROUP
    NT, CT, KT = S // P, G // P, D // P
    with ExitStack() as own_memory:
        sb = lambda n, s, t=F32: own_memory.enter_context(nc.sbuf_tensor(n, s, t))
        ps = lambda n, s: own_memory.enter_context(nc.psum_tensor(n, s, F32))
        w = sb("w_out_sb", [P, 2 * CT, D])
        x_row = sb("x_row", [P, 2, D])
        x2 = sb("x2_row", [P, 2, D])
        gain_fox, gain2 = sb("gain_fox", [P, G]), sb("gain2", [P, D])
        fox_rows = sb("fox_rows", [P, 2, G])
        foxT = sb("foxT", [P, 2, CT, P])
        squares_fox, squares = sb("squares_fox", [P, G]), sb("squares4", [P, D])
        h2_rows = sb("h2_rows", [P, 2, D])
        ssq_fox, ssq = sb("ssq_fox", [P, NT]), sb("ssq4", [P, NT])
        rfox, r2 = sb("rstd_fox", [P, NT]), sb("rstd2", [P, NT])
        turned_fox = ps("turned_fox", [P, CT, P])
        out_lru = ps("out_lru", [P, 2, HALF])
        out_fox = ps("out_fox", [P, 2, HALF])
        turned = ps("turned_h2", [P, KT, P])

        w_in, gains_in = sem("w_out_in"), sem("gains_in")
        x_in = [sem("x_row_in0"), sem("x_row_in1")]
        x2_stored = [sem("x2_stored0"), sem("x2_stored1")]
        fox_sum, fox_root, dve4 = sem("fox_sum"), sem("fox_root"), sem("dve4")
        fox_turned, foxT_done = sem("fox_turned"), sem("foxT_done")
        mixed, squared, rooted = sem("out_mixed"), sem("x2_squared"), sem("x2_rooted")
        h2_turned, h2_hi = sem("h2_turned"), sem("h2_hi")
        BEFORE, FOX, X2, VAR, ROWS, TILE = 3, 1, 3, 4, 6, 7

        with nc.Block() as block:
            @block.sync
            def _(sp):
                sp.dma_start(gain_fox[:], d.gn_fox_g.partition_broadcast(P)).then_inc(gains_in, 16)
                sp.wait_ge(gains_in, 16)
                sp.dma_start(gain2[:], d.norm2_g.partition_broadcast(P)).then_inc(gains_in, 16)
                sp.dma_start(w[:], d.w_out.rearrange("(k p) n -> p k n", p=P)).then_inc(w_in, 16)
                for b in range(NT):
                    if b >= 2:
                        sp.wait_ge(dve4, BEFORE + TILE * (b - 2) + X2)
                    sp.dma_start(x_row[:, b % 2], d.x[b * P:(b + 1) * P, :]).then_inc(x_in[b % 2], 16)
                    if b >= 2:
                        sp.dma_start(d.x2[(b - 2) * P:(b - 1) * P, :], x2[:, b % 2]).then_inc(x2_stored[b % 2], 16)
                for b in (NT - 2, NT - 1):
                    sp.wait_ge(dve4, BEFORE + TILE * b + X2)
                    sp.dma_start(d.x2[b * P:(b + 1) * P, :], x2[:, b % 2]).then_inc(x2_stored[b % 2], 16)
                sp.wait_ge(x2_stored[0], 16 * NT // 2)
                sp.wait_ge(x2_stored[1], 16 * NT // 2)

            @block.scalar
            def _(act):
                A = nc.scalar.activation
                for b in range(NT):
                    if b:
                        act.wait_ge(fox_sum, b)
                    A(squares_fox[:], m.fox[:, b, :], ACT.Square, accum_out=ssq_fox[:, b:b + 1]).then_inc(fox_sum, 1)
                act.wait_ge(dve4, 1)
                A(m.rstd_lru[:], m.rstd_lru[:], ACT.Sqrt).then_inc(fox_root, 1)
                A(ssq_fox[:], ssq_fox[:], ACT.Sqrt).then_inc(fox_root, 1)
                for b in range(NT):
                    act.wait_ge(fox_turned, b + 1)
                    A(foxT[:, b % 2], turned_fox[:], ACT.Copy).then_inc(foxT_done, 1)
                    act.wait_ge(dve4, BEFORE + TILE * b + X2)
                    if b:
                        act.wait_ge(squared, b)
                    A(squares[:], x2[:, b % 2], ACT.Square, accum_out=ssq[:, b:b + 1]).then_inc(squared, 1)
                    act.wait_ge(dve4, BEFORE + TILE * b + VAR)
                    A(r2[:, b:b + 1], r2[:, b:b + 1], ACT.Sqrt).then_inc(rooted, 1)
                    act.wait_ge(h2_turned, b + 1)
                    A(m.h2T[:, 0, :, b * P:(b + 1) * P], turned[:], ACT.Copy).then_inc(h2_hi, 1)

            @block.vector
            def _(dve):
                v = nc.vector
                own = Done(dve, dve4)
                dve.wait_ge(fox_sum, NT)
                own.link(v.tensor_scalar(ssq_fox[:], ssq_fox[:], 1.0 / G, EPS, ALU.mult, ALU.add))
                dve.wait_ge(fox_root, 2)
                own.mark(v.reciprocal(m.rstd_lru[:], m.rstd_lru[:]))
                own.link(v.reciprocal(rfox[:], ssq_fox[:]))
                dve.wait_ge(gains_in, 32)
                for b in range(NT):
                    s = b % 2
                    if b >= 1:
                        dve.wait_ge(mixed, b)
                    own.link(v.scalar_tensor_tensor(out=fox_rows[:, s], in0=m.fox[:, b, :], scalar=rfox[:, b:b + 1],
                                                    in1=gain_fox[:], op0=ALU.mult, op1=ALU.mult))
                    dve.wait_ge(mixed, b + 1)
                    dve.wait_ge(x_in[s], 16 * (b // 2 + 1))
                    if b >= 2:
                        dve.wait_ge(x2_stored[s], 16 * (b // 2))
                    own.link(v.scalar_tensor_tensor(out=x2[:, s], in0=out_lru[:].rearrange("p a b -> p (a b)"),
                                                    scalar=m.rstd_lru[:, b:b + 1], in1=x_row[:, s],
                                                    op0=ALU.mult, op1=ALU.add))
                    own.link(v.tensor_tensor(x2[:, s], x2[:, s], out_fox[:].rearrange("p a b -> p (a b)"), ALU.add))
                    dve.wait_ge(squared, b + 1)
                    own.mark(v.tensor_scalar(r2[:, b:b + 1], ssq[:, b:b + 1], 1.0 / D, EPS, ALU.mult, ALU.add))
                    dve.wait_ge(rooted, b + 1)
                    own.link(v.reciprocal(r2[:, b:b + 1], r2[:, b:b + 1]))
                    own.link(v.scalar_tensor_tensor(out=h2_rows[:, s], in0=x2[:, s], scalar=r2[:, b:b + 1],
                                                    in1=gain2[:], op0=ALU.mult, op1=ALU.mult))
                    dve.wait_ge(h2_hi, b + 1)
                    own.link(v.tensor_tensor(m.h2T[:, 1, :, b * P:(b + 1) * P], turned[:],
                                             m.h2T[:, 0, :, b * P:(b + 1) * P].bitcast(F32), ALU.subtract))
                assert own.count == BEFORE + TILE * NT

            @block.tensor
            def _(pe):
                pe.wait_ge(w_in, 16)
                for b in range(NT):
                    rows = slice(b * P, (b + 1) * P)
                    pe.wait_ge(dve4, BEFORE + TILE * b + FOX)
                    for c in range(CT):
                        last = nc.tensor.transpose(turned_fox[:, c], fox_rows[:, b % 2, c * P:(c + 1) * P], m.ident[:])
                    last.then_inc(fox_turned, 1)
                    for half, cols in enumerate(halves(2)):
                        for c in range(CT):
                            nc.tensor.matmul(out_lru[:, half], m.gateT[:, c, rows], w[:, c, cols],
                                             start=c == 0, stop=c == CT - 1)
                    pe.wait_ge(foxT_done, b + 1)
                    for half, cols in enumerate(halves(2)):
                        for c in range(CT):
                            last = nc.tensor.matmul(out_fox[:, half], foxT[:, b % 2, c], w[:, CT + c, cols],
                                                    start=c == 0, stop=c == CT - 1)
                    last.then_inc(mixed, 1)
                    pe.wait_ge(dve4, BEFORE + TILE * b + ROWS)
                    for k in range(KT):
                        last = nc.tensor.transpose(turned[:, k], h2_rows[:, b % 2, k * P:(k + 1) * P], m.ident[:])
                    last.then_inc(h2_turned, 1)


def score(nc, d, m, sem):
    D, S, NK = d.D, d.S, d.NK
    KT, NT, HP = D // P, S // P, 2 * d.PH
    with ExitStack() as own_memory:
        sb = lambda n, s, t=F32: own_memory.enter_context(nc.sbuf_tensor(n, s, t))
        ps = lambda n, s: own_memory.enter_context(nc.psum_tensor(n, s, F32))
        keys = sb("subkey_rows", [P, HP, P])
        keysT = sb("subkeysT", [P, HP, P])
        w = sb("wq_tile", [P, 2, KT, P])
        whi = sb("wq_hi", [P, 2, KT, P], F32R)
        wlo = sb("wq_lo", [P, 2, KT, P], F32R)
        qT = sb("peer_qT", [P, 2, S])
        rows = sb("score_rows", [P, 2, NT, NK])
        query = ps("query", [P, 2, HALF])
        score_ps = ps("score_ps", [P, 2, NT, NK])
        keys_ps = ps("keys_ps", [P, 4, P])

        keys_in = sem("keys_in")
        w_in = [sem("wq_in0"), sem("wq_in1")]
        stored = [sem("scores_stored0"), sem("scores_stored1")]
        keys_turned, keysT_done = sem("keys_turned"), sem("keysT_done")
        hi_done, lo_done = sem("wq_hi_done"), sem("wq_lo_done")
        query_done, query_read = sem("query_done"), sem("query_read")
        scored, scores_read, apart = sem("scored"), sem("scores_read"), sem("score_waits")

        with nc.Block() as block:
            @block.sync
            def _(sp):
                sp.dma_start(keys[:], d.peer_subkeys.rearrange("h n c -> n h c")).then_inc(keys_in, 16)
                with sp.Fori(0, HP // 2) as i:
                    for b in range(2):
                        sp.wait_ge(lo_done, 2 * i + 1)
                        sp.dma_start(w[:, b], d.peer_wq[:, bass.ds((2 * i + b) * P, P)]
                                     .rearrange("(k p) n -> p k n", p=P)).then_inc(w_in[b], 16)

            @block.gpsimd
            def _(pool):
                with pool.Fori(0, HP // 2) as i:
                    for b in range(2):
                        pool.wait_ge(w_in[b], 16 * (i + 1))
                        pool.wait_ge(query_done, (2 * i + b) * 2 + 1)
                        pool.sem_inc(apart, 1)
                        pool.tensor_copy(whi[:, b], w[:, b]).then_inc(hi_done, 1)

            @block.vector
            def _(dve):
                dve.sem_inc(lo_done, 1)
                with dve.Fori(0, HP // 2) as i:
                    for b in range(2):
                        dve.wait_ge(hi_done, 2 * i + b + 1)
                        nc.vector.tensor_tensor(wlo[:, b], w[:, b], whi[:, b].bitcast(F32), ALU.subtract
                                                ).then_inc(lo_done, 1)

            @block.tensor
            def _(pe):
                pe.wait_ge(keys_in, 16)
                for g in range(HP // 4):
                    if g:
                        pe.wait_ge(keysT_done, g)
                    for j in range(4):
                        last = nc.tensor.transpose(keys_ps[:, j], keys[:, 4 * g + j, :], m.ident[:])
                    last.then_inc(keys_turned, 1)
                pe.wait_ge(keysT_done, HP // 4)
                pe.sem_inc(query_done, 3)
                with pe.Fori(0, HP // 2) as i:
                    for b in range(2):
                        pe.wait_ge(lo_done, 2 * i + b + 2)
                        for half, cols in enumerate(halves(2)):
                            pe.wait_ge(query_read, (2 * i + b) * 2 + half + 1)
                            for n, (part, t) in enumerate([(whi, 0), (whi, 1), (wlo, 0)]):
                                for k in range(KT):
                                    last = nc.tensor.matmul(query[:, half], part[:, b, k], m.h2T[:, t, k, cols],
                                                            start=n == 0 and k == 0, stop=n == 2 and k == KT - 1)
                            last.then_inc(query_done, 1)
                        pe.wait_ge(query_read, (2 * i + b) * 2 + 4)
                        pe.wait_ge(scores_read, 2 * i + b + 1)
                        for t in range(NT):
                            last = nc.tensor.matmul(score_ps[:, b, t], qT[:, b, t * P:(t + 1) * P],
                                                    keysT[:, bass.ds(2 * i + b, 1), :].rearrange("p a n -> p (a n)"),
                                                    start=True, stop=True)
                        last.then_inc(scored, 1)

            @block.scalar
            def _(act):
                A = nc.scalar.activation
                for g in range(HP // 4):
                    act.wait_ge(keys_turned, g + 1)
                    A(keysT[:, 4 * g:4 * g + 4, :], keys_ps[:], ACT.Copy).then_inc(keysT_done, 1)
                act.sem_inc(query_read, 2)
                act.sem_inc(scores_read, 2)
                act.sem_inc(stored[0], 16)
                act.sem_inc(stored[1], 16)
                with act.Fori(0, HP // 2) as i:
                    for b in range(2):
                        for half, cols in enumerate(halves(2)):
                            act.wait_ge(query_done, (2 * i + b) * 2 + half + 4)
                            A(qT[:, b, cols], query[:, half], ACT.Copy).then_inc(query_read, 1)
                        act.wait_ge(scored, 2 * i + b + 1)
                        act.wait_ge(stored[b], 16 * i + 16)
                        A(rows[:, b], score_ps[:, b], ACT.Copy).then_inc(scores_read, 1)
                        act.wait_ge(scores_read, 2 * i + b + 3)
                        act.dma_start(d.scores[:, :, bass.ds(2 * i + b, 1), :].rearrange("t p a n -> p t (a n)"),
                                      rows[:, b]).then_inc(stored[b], 16)
                act.wait_ge(stored[0], 16 * (HP // 2) + 16)
                act.wait_ge(stored[1], 16 * (HP // 2) + 16)


def experts_up(nc, d, m, sem):
    D, S, NK, PH, TOP = d.D, d.S, d.NK, d.PH, d.TOP
    KT, NT = D // P, S // P
    FIRST, STEPS = 16, 14
    assert FIRST + NT * STEPS == NK and FIRST % 2 == 0 and STEPS % 2 == 0
    GROUP = 4
    GROUPS = P // GROUP
    SLOTS = 4
    u_rows = d.peer_u.rearrange("(p e) n -> p e n", p=NK)
    with ExitStack() as own_memory:
        sb = lambda n, s, t=F32: own_memory.enter_context(nc.sbuf_tensor(n, s, t))
        ps = lambda n, s: own_memory.enter_context(nc.psum_tensor(n, s, F32))
        u = sb("u_chunk", [P, 2, D])
        uhi = sb("uT_hi", [P, 2, KT, P], F32R)
        ulo = sb("uT_lo", [P, 2, KT, P], F32R)
        act_out = sb("expert_acts", [P, 2, S])
        first_hot = sb("first_hot", [P, SLOTS, GROUP, NK])
        second_hot = sb("second_hot", [P, SLOTS, GROUP, NK])
        spread = sb("gates_spread", [P, 2, NK, P // 2])
        sc = sb("scores_tile", [P, 2 * PH, NK])
        rest = sb("scores_rest", [P, 2, NK])
        val = sb("top_values", [P, PH, 2, TOP])
        idx = sb("top_indices", [P, PH, 2, TOP], U32)
        cand = sb("pair_scores", [P, TOP, TOP])
        crest = sb("pair_rest", [P, TOP * TOP])
        pval = sb("pair_values", [P, PH, TOP])
        pidx = sb("pair_indices", [P, PH, TOP], U32)
        pdig = sb("pair_digits", [P, 2, PH, TOP], U32)
        idxf = sb("top_indices_f", [P, PH, 2, TOP])
        pdigf = sb("pair_digits_f", [P, 2, PH, TOP])
        hot = sb("rank_hot", [P, PH * TOP, TOP])
        route = sb("route", [P, 3, PH, TOP])
        gsum = sb("gate_sums", [P, PH])
        routeT = sb("routeT", [P, 3, P])
        turned = ps("u_turned_ps", [P, KT, P])
        pre = ps("expert_pre", [P, 2, HALF])
        spread_ps = ps("spread_ps", [P, 2, GROUP, NK])
        route_ps = ps("route_ps", [P, 3, P])

        u_in = [sem("u_in0"), sem("u_in1")]
        sc_in, sc_used = sem("scores_tile_in"), sem("scores_tile_used")
        u_turned, hi_done, lo_done = sem("u_turned"), sem("u_hi_done"), sem("u_lo_done")
        pre_done, act_done = sem("pre_done"), sem("expert_act_done")
        act_stored = [sem("act_stored0"), sem("act_stored1")]
        hot_done, spread_done, spread_read = sem("hot_done"), sem("spread_done"), sem("spread_read")
        spread_stored = [sem("spread_stored0"), sem("spread_stored1")]
        picked = sem("route_step")
        shifted, exp_done = sem("pairs_shifted"), sem("pairs_exp")
        route_done, route_turned, routeT_done = sem("route_done"), sem("route_turned"), sem("routeT_done")

        HEAD_STEPS = 16
        TILE_STEPS = PH * HEAD_STEPS + 12

        def passes(engine, body):
            body(0, None, 0)
            with engine.Fori(0, NT - 1) as i:
                body(FIRST + STEPS * i, i, i + 1)
            body(FIRST + STEPS * (NT - 1), NT - 1, None)

        def groups_of(step):
            return range(step * GROUPS // STEPS, (step + 1) * GROUPS // STEPS)

        def steps_of(tile):
            return FIRST if tile is None else STEPS

        def slot_turns(chunk0, tile):
            if isinstance(chunk0, int):
                return chunk0 // 2
            return FIRST // 2 + (STEPS // 2) * tile

        with nc.Block() as block:
            @block.sync
            def _(sp):
                def body(c0, tile, select):
                    for s in range(steps_of(tile)):
                        if s == 1 and select is not None:
                            sp.wait_ge(sc_used, select)
                            sp.dma_start(sc[:], d.scores[bass.ds(select, 1)].rearrange("a p h n -> p (a h) n")
                                         ).then_inc(sc_in, 16)
                        sp.wait_ge(u_turned, c0 + s)
                        sp.dma_start(u[:, s % 2], u_rows[:, bass.ds(c0 + s, 1), :].rearrange("p a n -> p (a n)")
                                     ).then_inc(u_in[s % 2], 16)
                passes(sp, body)

            @block.tensor
            def _(pe):
                pe.sem_inc(u_turned, 1)
                pe.sem_inc(pre_done, 2)
                pe.sem_inc(spread_done, SLOTS)

                def turn(chunk, s, turns):
                    pe.wait_ge(u_in[s % 2], 16 * (turns + 1))
                    pe.wait_ge(lo_done, chunk)
                    for k in range(KT):
                        last = nc.tensor.transpose(turned[:, k], u[:, s % 2, k * P:(k + 1) * P], m.ident[:])
                    last.then_inc(u_turned, 1)

                def multiply(chunk, s, half, cols):
                    pe.wait_ge(act_done, 2 * chunk + half)
                    for n, (part, t) in enumerate([(uhi, 0), (uhi, 1), (ulo, 0)]):
                        for k in range(KT):
                            last = nc.tensor.matmul(pre[:, half], part[:, s % 2, k], m.h2T[:, t, k, cols],
                                                    start=n == 0 and k == 0, stop=n == 2 and k == KT - 1)
                    last.then_inc(pre_done, 1)

                def spread_group(tile, g):
                    pe.wait_ge(hot_done, tile * GROUPS + g + 1)
                    pe.wait_ge(spread_read, tile * GROUPS + g + 1)
                    for j in range(GROUP):
                        last = nc.tensor.matmul(spread_ps[:, g % 2, j], first_hot[:, g % SLOTS, j],
                                                second_hot[:, g % SLOTS, j], start=True, stop=True)
                    last.then_inc(spread_done, 1)

                turn(0, 0, 0)

                def body(c0, tile, select):
                    turns, steps = slot_turns(c0, tile), steps_of(tile)
                    for s in range(steps):
                        if s + 1 < steps or select is not None:
                            turn(c0 + s + 1, s + 1, turns + (s + 1) // 2)
                        pe.wait_ge(lo_done, c0 + s + 1)
                        groups = [] if tile is None else list(groups_of(s))
                        multiply(c0 + s, s, 0, slice(0, HALF))
                        for g in groups[:1]:
                            spread_group(tile, g)
                        multiply(c0 + s, s, 1, slice(HALF, 2 * HALF))
                        for g in groups[1:]:
                            spread_group(tile, g)
                        if s == STEPS - 1 and select is not None:
                            pe.wait_ge(route_done, select + 1)
                            for n in range(3):
                                last = nc.tensor.transpose(route_ps[:, n], route[:, n].rearrange("p a b -> p (a b)"),
                                                           m.ident[:])
                            last.then_inc(route_turned, 1)
                passes(pe, body)

            @block.scalar
            def _(act):
                A = nc.scalar.activation
                act.sem_inc(act_done, 1)
                act.sem_inc(spread_read, 2)
                act.sem_inc(spread_stored[0], 16)
                act.sem_inc(spread_stored[1], 16)

                def high(chunk, s):
                    act.wait_ge(u_turned, chunk + 2)
                    act.wait_ge(pre_done, 2 * chunk)
                    A(uhi[:, s % 2], turned[:], ACT.Copy).then_inc(hi_done, 1)

                def spread_out(tile, g):
                    part, col = divmod(g, GROUPS // 2)
                    act.wait_ge(spread_done, tile * GROUPS + g + 1 + SLOTS)
                    if col == 0:
                        act.wait_ge(spread_stored[part], 16 * tile + 16)
                    A(spread[:, part, :, col * GROUP:(col + 1) * GROUP].rearrange("p e t -> p t e"),
                      spread_ps[:, g % 2], ACT.Copy).then_inc(spread_read, 1)
                    if col == GROUPS // 2 - 1:
                        act.wait_ge(spread_read, tile * GROUPS + g + 3)
                        act.dma_start(d.gates[bass.ds(2 * tile + part, 1)].rearrange("a p e t -> p (a e t)"),
                                      spread[:, part].rearrange("p e t -> p (e t)")).then_inc(spread_stored[part], 16)

                high(0, 0)

                def body(c0, tile, select):
                    turns, steps = slot_turns(c0, tile), steps_of(tile)
                    for s in range(steps):
                        if s + 1 < steps or select is not None:
                            high(c0 + s + 1, s + 1)
                        groups = [] if tile is None else list(groups_of(s))
                        for half in range(2):
                            act.wait_ge(pre_done, 2 * (c0 + s) + half + 3)
                            if half == 0:
                                act.wait_ge(act_stored[s % 2], 16 * (turns + s // 2))
                            A(act_out[:, s % 2, half * HALF:(half + 1) * HALF], pre[:, half], ACT.Gelu_apprx_tanh
                              ).then_inc(act_done, 1)
                            for g in (groups[:1], groups[1:])[half]:
                                spread_out(tile, g)
                        act.wait_ge(act_done, 2 * (c0 + s) + 3)
                        act.dma_start(d.acts[bass.ds(c0 + s, 1)].rearrange("a p t -> p (a t)"), act_out[:, s % 2]
                                      ).then_inc(act_stored[s % 2], 16)
                        if s == 11 and select is not None:
                            act.wait_ge(shifted, select + 1)
                            A(route[:, 2], route[:, 2], ACT.Exp).then_inc(exp_done, 1)
                passes(act, body)
                for b in range(2):
                    act.wait_ge(act_stored[b], 16 * (NK // 2))
                    act.wait_ge(spread_stored[b], 16 * NT + 16)

            @block.vector
            def _(dve):
                v = nc.vector
                own = Done(dve, picked)
                iota = m.iota[:, 0:TOP]

                def low(chunk, s):
                    dve.wait_ge(hi_done, chunk + 1)
                    v.tensor_tensor(ulo[:, s % 2], turned[:], uhi[:, s % 2].bitcast(F32), ALU.subtract
                                    ).then_inc(lo_done, 1)

                def hot_group(tile, g):
                    dve.wait_ge(spread_done, tile * GROUPS + g + 1)
                    for j in range(GROUP):
                        t = g * GROUP + j
                        v.tensor_scalar(first_hot[:, g % SLOTS, j], m.iota[:], routeT[:, 0, t:t + 1], None, ALU.is_equal)
                        last = v.tensor_scalar(second_hot[:, g % SLOTS, j], m.iota[:], routeT[:, 1, t:t + 1],
                                               routeT[:, 2, t:t + 1], ALU.is_equal, ALU.mult)
                    last.then_inc(hot_done, 1)

                apart = sem("select_waits")

                def top(values, indices, source, left):
                    own.link_apart(v.max(values[:, 0:8], source), apart)
                    own.mark(v.max_index(indices[:, 0:8], values[:, 0:8], source))
                    own.link_apart(v.match_replace(left, values[:, 0:8], source, LOWEST), apart)
                    own.link_apart(v.max(values[:, 8:16], left), apart)
                    own.link_apart(v.max_index(indices[:, 8:16], values[:, 8:16], left), apart)

                def select_head(h):
                    for p in range(2):
                        top(val[:, h, p], idx[:, h, p], sc[:, 2 * h + p, :], rest[:, p])
                    own.link(v.tensor_tensor(cand[:], val[:, h, 0].rearrange("p (a b) -> p a b", b=1)
                                             .to_broadcast([P, TOP, TOP]),
                                             val[:, h, 1].rearrange("p (a b) -> p a b", a=1)
                                             .to_broadcast([P, TOP, TOP]), ALU.add))
                    dve.sem_inc(apart, 1)
                    top(pval[:, h], pidx[:, h], cand[:].rearrange("p a b -> p (a b)"), crest[:])

                def digits():
                    own.mark(v.tensor_scalar(pdig[:, 0], pidx[:], TOP.bit_length() - 1, None, ALU.logical_shift_right))
                    own.mark(v.tensor_scalar(pdig[:, 1], pidx[:], TOP - 1, None, ALU.bitwise_and))
                    own.link(v.tensor_copy(idxf[:], idx[:]))
                    own.link(v.tensor_copy(pdigf[:], pdig[:]))

                def key(p):
                    flat = pdigf[:, p].rearrange("p h (k a) -> p (h k) a", a=1)
                    own.link(v.tensor_tensor(hot[:], flat.to_broadcast([P, PH * TOP, TOP]),
                                             iota.rearrange("p (a b) -> p a b", a=1)
                                             .to_broadcast([P, PH * TOP, TOP]), ALU.is_equal))
                    own.link(v.tensor_tensor(hot[:].rearrange("p (h k) r -> p h k r", h=PH),
                                             hot[:].rearrange("p (h k) r -> p h k r", h=PH),
                                             idxf[:, :, p].rearrange("p h (a r) -> p h a r", a=1)
                                             .to_broadcast([P, PH, TOP, TOP]), ALU.mult))
                    own.link(v.tensor_reduce(route[:, p].rearrange("p h k -> p (h k)"), hot[:], AX_X, ALU.add))

                def body(c0, tile, select):
                    steps = steps_of(tile)
                    if tile is not None:
                        dve.wait_ge(route_turned, tile + 1)
                        v.tensor_copy(routeT[:], route_ps[:]).then_inc(routeT_done, 1)
                        dve.wait_ge(routeT_done, tile + 1)
                    if select is not None:
                        own.enter(select, TILE_STEPS)
                    for s in range(steps):
                        if s + 1 < steps or select is not None:
                            low(c0 + s + 1, s + 1)
                        if tile is not None:
                            for g in groups_of(s):
                                hot_group(tile, g)
                        if select is None:
                            continue
                        if s == 1:
                            dve.wait_ge(sc_in, 16 * (select + 1))
                            dve.sem_inc(apart, 1)
                        if 1 <= s <= PH:
                            select_head(s - 1)
                        if s == PH:
                            dve.sem_inc(sc_used, 1)
                        if s == 9:
                            digits()
                            if tile is not None:
                                dve.wait_ge(route_turned, select)
                            key(0)
                        if s == 10:
                            key(1)
                            v.tensor_tensor(route[:, 2], pval[:], pval[:, :, 0:1].to_broadcast([P, PH, TOP]), ALU.subtract
                                            ).then_inc(shifted, 1)
                        if s == 12:
                            dve.wait_ge(exp_done, select + 1)
                            own.link(v.tensor_reduce(gsum[:], route[:, 2], AX_X, ALU.add))
                            own.link(v.reciprocal(gsum[:], gsum[:]))
                            v.tensor_tensor(route[:, 2], route[:, 2],
                                            gsum[:].rearrange("p (h a) -> p h a", a=1).to_broadcast([P, PH, TOP]),
                                            ALU.mult).then_inc(route_done, 1)
                            assert own.count == TILE_STEPS, own.count

                dve.wait_ge(hi_done, 1)
                low(0, 0)
                passes(dve, body)


def experts_down(nc, d, m, sem):
    D, S, NK = d.D, d.S, d.NK
    NT = S // P
    C = 2
    BANKS = NT * D // HALF
    RING = 8
    v_rows = d.peer_v.rearrange("(p e) n -> p e n", p=NK)
    PASSES = NK // C // 2
    with ExitStack() as own_memory:
        sb = lambda n, s, t=F32: own_memory.enter_context(nc.sbuf_tensor(n, s, t))
        prod = sb("acts_times_gates", [P, 2, C, S])
        gate = sb("gates_group", [P, 2, 2 * NT, C, P // 2])
        vt = sb("v_group", [P, 2, C, D])
        whi, wlo = sb("w_hi", [P, 2, C, S], F32R), sb("w_lo", [P, 2, C, S], F32R)
        vhi, vlo = sb("v_hi", [P, 2, C, D], F32R), sb("v_lo", [P, 2, C, D], F32R)
        out = own_memory.enter_context(nc.psum_tensor("expert_out", [P, RING, HALF], F32))

        y_in = sem("x2_in")
        a_in, g_in, v_in = ([sem(f"{n}_in{b}") for b in range(2)] for n in ("acts", "gates", "v"))
        prod_done, whi_done, wlo_done = sem("prod_done"), sem("w_hi_done"), sem("w_lo_done")
        vhi_done, vlo_done = sem("v_hi_done"), sem("v_lo_done")
        out_done, out_read = sem("expert_out_done"), sem("expert_out_read")

        with nc.Block() as block:
            @block.sync
            def _(sp):
                sp.dma_start(m.y[:], d.x2.rearrange("(t p) n -> p t n", p=P)).then_inc(y_in, 16)
                with sp.Fori(0, PASSES) as i:
                    for b in range(2):
                        n = 2 * i + b
                        sp.wait_ge(wlo_done, C * n + 1)
                        sp.dma_start(prod[:, b], d.acts[bass.ds(C * n, C)].rearrange("c p t -> p c t")
                                     ).then_inc(a_in[b], 16)
                        sp.dma_start(gate[:, b], d.gates[:, :, bass.ds(C * n, C), :].rearrange("t p c k -> p t c k")
                                     ).then_inc(g_in[b], 16)
                        sp.wait_ge(vlo_done, C * n + 1)
                        sp.dma_start(vt[:, b], v_rows[:, bass.ds(C * n, C), :]).then_inc(v_in[b], 16)

            @block.gpsimd
            def _(pool):
                pool.sem_inc(vlo_done, C + 1)
                with pool.Fori(0, PASSES) as i:
                    for b in range(2):
                        for c in range(C):
                            pool.wait_ge(vhi_done, (2 * i + b) * C + c + 1)
                            pool.tensor_tensor(vlo[:, b, c], vt[:, b, c], vhi[:, b, c].bitcast(F32), ALU.subtract
                                               ).then_inc(vlo_done, 1)

            @block.scalar
            def _(act):
                with act.Fori(0, PASSES) as i:
                    for b in range(2):
                        n = 2 * i + b
                        act.wait_ge(out_done, BANKS * n + 1)
                        act.wait_ge(v_in[b], 16 * (i + 1))
                        for c in range(C):
                            nc.scalar.activation(vhi[:, b, c], vt[:, b, c], ACT.Copy).then_inc(vhi_done, 1)
                        for c in range(C):
                            act.wait_ge(prod_done, C * n + c + 1)
                            nc.scalar.activation(whi[:, b, c], prod[:, b, c], ACT.Copy).then_inc(whi_done, 1)

            @block.vector
            def _(dve):
                v = nc.vector
                dve.sem_inc(wlo_done, C + 1)
                dve.sem_inc(out_read, RING)

                def multiply(i, b):
                    dve.wait_ge(a_in[b], 16 * (i + 1))
                    dve.wait_ge(g_in[b], 16 * (i + 1))
                    for c in range(C):
                        tokens = prod[:, b, c].rearrange("p (t k) -> p t k", k=P // 2)
                        v.tensor_tensor(tokens, tokens, gate[:, b, :, c, :], ALU.mult).then_inc(prod_done, 1)

                def low(n, b, c):
                    dve.wait_ge(whi_done, C * n + c + 1)
                    v.tensor_tensor(wlo[:, b, c], prod[:, b, c], whi[:, b, c].bitcast(F32), ALU.subtract
                                    ).then_inc(wlo_done, 1)

                def add(n, j):
                    t, half = divmod(j, 2)
                    dve.wait_ge(out_done, BANKS * n + j + 2 + BANKS)
                    cols = slice(half * HALF, (half + 1) * HALF)
                    v.tensor_tensor(m.y[:, t, cols], m.y[:, t, cols], out[:, j % RING], ALU.add).then_inc(out_read, 1)

                def prepare_beside_adds(i, b):
                    n = 2 * i + b
                    multiply(i, b)
                    for j in range(BANKS):
                        if j in (2, 4):
                            low(n, b, j // 2 - 1)
                        add(n - 1, j)

                multiply(0, 0)
                for c in range(C):
                    low(0, 0, c)
                dve.wait_ge(y_in, 16)
                prepare_beside_adds(0, 1)
                with dve.Fori(1, PASSES) as i:
                    for b in range(2):
                        prepare_beside_adds(i, b)
                for j in range(BANKS):
                    add(NK // C - 1, j)

            @block.tensor
            def _(pe):
                pe.sem_inc(out_done, BANKS + 1)
                with pe.Fori(0, PASSES) as i:
                    for b in range(2):
                        n = 2 * i + b
                        pe.wait_ge(wlo_done, C * n + 2 * C + 1)
                        pe.wait_ge(vlo_done, C * n + 2 * C + 1)
                        for j in range(BANKS):
                            t, half = divmod(j, 2)
                            rows, cols = slice(t * P, (t + 1) * P), slice(half * HALF, (half + 1) * HALF)
                            pe.wait_ge(out_read, BANKS * n + j + 1)
                            terms = [(a, e, c) for c in range(C) for a, e in ((whi, vhi), (whi, vlo), (wlo, vhi))]
                            for k, (a, e, c) in enumerate(terms):
                                last = nc.tensor.matmul(out[:, j % RING], a[:, b, c, rows], e[:, b, c, cols],
                                                        start=k == 0, stop=k == len(terms) - 1)
                            last.then_inc(out_done, 1)


def last_norm(nc, d, m, sem):
    D, NT = d.D, d.S // P
    with ExitStack() as own_memory:
        sb = lambda n, s, t=F32: own_memory.enter_context(nc.sbuf_tensor(n, s, t))
        gain, squares = sb("gain_last", [P, D]), sb("squares8", [P, 2, D])
        sums = sb("sums8", [P, NT])
        rows = sb("normed_rows", [P, NT, D])
        gain_in, summed, dve8, rooted = sem("gain8_in"), sem("y_summed"), sem("dve8"), sem("y_rooted")
        stored = [sem(f"out_stored{b}") for b in range(NT)]

        with nc.Block() as block:
            @block.sync
            def _(sp):
                sp.dma_start(gain[:], d.final_g.partition_broadcast(P)).then_inc(gain_in, 16)
                for b in range(NT):
                    sp.wait_ge(dve8, 2 + b + 1)
                    sp.dma_start(d.out[b * P:(b + 1) * P, :], rows[:, b, :]).then_inc(stored[b], 16)
                for b in range(NT):
                    sp.wait_ge(stored[b], 16)

            @block.scalar
            def _(act):
                for b in range(NT):
                    if b >= 2:
                        act.wait_ge(summed, b - 1)
                    nc.scalar.activation(squares[:, b % 2], m.y[:, b, :], ACT.Square, accum_out=sums[:, b:b + 1]
                                         ).then_inc(summed, 1)
                act.wait_ge(dve8, 1)
                nc.scalar.activation(sums[:], sums[:], ACT.Sqrt).then_inc(rooted, 1)

            @block.vector
            def _(dve):
                v = nc.vector
                own = Done(dve, dve8)
                dve.wait_ge(summed, NT)
                own.link(v.tensor_scalar(sums[:], sums[:], 1.0 / D, EPS, ALU.mult, ALU.add))
                dve.wait_ge(rooted, 1)
                own.link(v.reciprocal(sums[:], sums[:]))
                dve.wait_ge(gain_in, 16)
                for b in range(NT):
                    own.mark(v.scalar_tensor_tensor(out=rows[:, b, :], in0=m.y[:, b, :], scalar=sums[:, b:b + 1],
                                                    in1=gain[:], op0=ALU.mult, op1=ALU.mult))


def hybrid_block(nc, args, stop=None):
    d = Parts()
    d.x, d.norm1_g, d.w_in, d.conv_w = (args["x"], args["norm1_g"], args["w_in"], args["conv_w"])
    d.conv_b, d.lru_wa, d.lru_ba, d.lru_wx = (args["conv_b"], args["lru_wa"], args["lru_ba"], args["lru_wx"])
    d.lru_bx, d.lru_lambda, d.fox_bf, d.gn_lru_g = (args["lru_bx"], args["lru_lambda"], args["fox_bf"], args["gn_lru_g"])
    d.gn_fox_g, d.w_out, d.norm2_g, d.peer_wq = (args["gn_fox_g"], args["w_out"], args["norm2_g"], args["peer_wq"])
    d.peer_subkeys, d.peer_u, d.peer_v, d.final_g = (args["peer_subkeys"], args["peer_u"], args["peer_v"], args["final_g"])
    d.out = args["out"]
    d.S, d.D = d.x.shape
    d.GROUP, d.TAPS, d.FH = d.D // 2, d.conv_w.shape[0], d.fox_bf.shape[0]
    d.PAD = d.TAPS - 1
    d.LHD, d.FHD = d.lru_wa.shape[1], d.GROUP // d.FH
    d.QSCALE = float(d.FHD) ** -0.5
    d.PH, d.NK, d.TOP = d.peer_subkeys.shape[0] // 2, d.peer_subkeys.shape[1], 16
    NT, CT, KT = d.S // P, d.GROUP // P, d.D // P
    scratch = lambda n, s: nc.dram_tensor(n, s, F32, kind="Internal").ap()
    d.x2 = scratch("x2_dram", [d.S, d.D])
    d.scores = scratch("scores_dram", [NT, P, 2 * d.PH, d.NK])
    d.acts = scratch("acts_dram", [d.NK, d.NK, d.S])
    d.gates = scratch("gates_dram", [2 * NT, d.NK, d.NK, P // 2])

    with ExitStack() as memory:
        def sem(name):
            return memory.enter_context(nc.semaphore(name))

        m = Parts()
        m.d = d
        sb = lambda stack, n, s, t=F32, **k: stack.enter_context(nc.sbuf_tensor(n, s, t, **k))
        m.ident = sb(memory, "ident", [P, P])
        m.iota = sb(memory, "iota", [P, P])
        m.ones_col = sb(memory, "ones_col", [P, 1])
        m.rstd_lru = sb(memory, "rstd_lru", [P, NT])

        m.ident_ready = sem("ident_ready")
        with nc.Block() as block:
            @block.gpsimd
            def _(pool):
                pool.memset(m.ident[:], 0.0).then_inc(m.ident_ready, 1)
                pool.wait_ge(m.ident_ready, 1)
                pool.affine_select(out=m.ident[:], in_=m.ident[:], compare_op=ALU.not_equal, fill=1.0, base=0,
                                   pattern=[[-1, P]], channel_multiplier=1).then_inc(m.ident_ready, 1)
                pool.iota(m.iota[:], [[1, P]], base=0, channel_multiplier=0, allow_small_or_imprecise_dtypes=True)
                pool.memset(m.ones_col[:], 1.0)

        with ExitStack() as groups:
            m.gateT = sb(groups, "gateT", [P, CT, d.S])
            conv_row = d.PAD + d.S
            shared = sb(groups, "x_proj_then_attention", [P, CT * conv_row])
            m.xrT = shared[:].rearrange("p (c s) -> p c s", s=conv_row)
            m.fox = shared[:, 0:NT * d.GROUP].rearrange("p (t n) -> p t n", n=d.GROUP)
            with ExitStack() as heads:
                m.qT = sb(heads, "qT", [P, CT, d.S])
                m.kT = sb(heads, "kT", [P, CT, d.S])
                m.v = sb(heads, "v_heads", [P, NT, d.GROUP])
                m.forget = sb(heads, "forget", [d.FH, d.S])
                project(nc, d, m, sem)
                if stop == "project": return m
                recur(nc, d, m, sem)
                if stop == "recur": return m
                attend(nc, d, m, sem)
                if stop == "attend": return m
            h2 = ExitStack()
            m.h2T = sb(h2, "h2T", [P, 2, KT, d.S], F32R, side="right")
            mix_out(nc, d, m, sem)
        if stop == "mix": return m
        with h2:
            score(nc, d, m, sem)
            if stop == "score": return m
            experts_up(nc, d, m, sem)
        if stop == "up": return m
        m.y = sb(memory, "y", [P, NT, d.D])
        experts_down(nc, d, m, sem)
        last_norm(nc, d, m, sem)


_INS = ["x", "norm1_g", "w_in", "conv_w", "conv_b", "lru_wa", "lru_ba", "lru_wx", "lru_bx", "lru_lambda", "fox_bf",
        "gn_lru_g", "gn_fox_g", "w_out", "norm2_g", "peer_wq", "peer_subkeys", "peer_u", "peer_v", "final_g"]


def kernel(**inputs):
    import numpy as _np
    import concourse.bacc as _bacc
    from concourse.bass_utils import run_bass_kernel_spmd as _run

    nc = _bacc.Bacc("TRN2", target_bir_lowering=False, num_devices=1)
    arrays, args = {}, {}
    for name in _INS:
        a = _np.ascontiguousarray(inputs[name])
        if name != "final_g":
            a = a.reshape(a.shape[1:])
        if name == "peer_subkeys":
            a = a.reshape((-1,) + a.shape[2:])
        arrays[f"in_{name}"] = a
        args[name] = nc.dram_tensor(f"in_{name}", a.shape, mybir.dt.from_np(a.dtype), kind="ExternalInput").ap()
    shape = inputs["x"].shape
    args["out"] = nc.dram_tensor("out_rows", shape[1:], F32, kind="ExternalOutput").ap()
    hybrid_block(nc, args)
    r = _run(nc, [arrays], core_ids=[0])
    return r.results[0]["out_rows"].reshape(shape)
```

```python
from contextlib import ExitStack
import concourse.bass as bass
from concourse import mybir

ALU = mybir.AluOpType
ACT = mybir.ActivationFunctionType
AX_X = mybir.AxisListType.X
F32 = mybir.dt.float32
F32R = mybir.dt.float32r
U32 = mybir.dt.uint32
I32 = mybir.dt.int32

P = 128
HALF = 512
EPS = 1e-6
LRU_C = 8.0
BIG = 1e30
LOWEST = -3.0e38
LOG1P_TERMS = 8


class Parts:
    pass


class Done:

    def __init__(self, engine, semaphore):
        self.engine, self.semaphore, self.count, self.base = engine, semaphore, 0, 0

    def mark(self, instruction):
        instruction.then_inc(self.semaphore, 1)
        self.count += 1
        return self.count

    def wait(self, count):
        self.engine.wait_ge(self.semaphore, self.base + count)

    def link(self, instruction):
        self.wait(self.mark(instruction))

    def link_apart(self, instruction, count_waits):
        self.link(instruction)
        self.engine.sem_inc(count_waits, 1)

    def enter(self, i, per_pass):
        self.count, self.base = 0, i * per_pass


def halves(n=2):
    return [slice(h * HALF, (h + 1) * HALF) for h in range(n)]


def log1p_series(dve, own, e, s, s2, acc):
    own.link(dve.tensor_scalar(s, e, 2.0, None, ALU.add))
    own.link(dve.reciprocal(s, s))
    own.link(dve.tensor_tensor(s, s, e, ALU.mult))
    own.link(dve.tensor_tensor(s2, s, s, ALU.mult))
    own.link(dve.tensor_scalar(acc, s2, 1.0 / (2 * LOG1P_TERMS - 1), None, ALU.mult))
    for n in range(LOG1P_TERMS - 2, 0, -1):
        own.link(dve.scalar_tensor_tensor(out=acc, in0=acc, scalar=1.0 / (2 * n + 1), in1=s2,
                                          op0=ALU.add, op1=ALU.mult))
    own.link(dve.tensor_scalar(acc, acc, 1.0, 2.0, ALU.add, ALU.mult))
    own.link(dve.tensor_tensor(acc, acc, s, ALU.mult))


def project(nc, d, m, sem):
    D, S, G = d.D, d.S, d.GROUP
    KT, NT, CT = D // P, S // P, G // P
    HD = d.LHD
    with ExitStack() as own_memory:
        sb = lambda n, s, t=F32: own_memory.enter_context(nc.sbuf_tensor(n, s, t))
        ps = lambda n, s: own_memory.enter_context(nc.psum_tensor(n, s, F32))
        x_rows = m.qk[:].rearrange("p a c s -> p (a c s)").rearrange("p (t n) -> p t n", n=D)
        gain = sb("gain1", [P, D])
        h_rows = sb("h_rows", [P, 2, D])
        hT = m.hT
        w = sb("w_in_group", [P, 2, KT, G])
        wf = sb("w_forget", [P, KT, d.FH])
        squares = sb("squares1", [P, D])
        sums = sb("sums1", [P, NT])
        rstd = sb("rstd1", [P, NT])
        fbias = sb("forget_bias", [d.FH, 1])
        turned = ps("turned1", [P, 2, KT, P])
        product = ps("product1", [P, 4, HALF])

        x_in = [sem(f"x_in{b}") for b in range(NT)]
        small_in, gain_in = sem("small1_in"), sem("gain1_in")
        w_in = [sem("w_in0"), sem("w_in1")]
        summed, rooted, dve1 = sem("x_summed"), sem("x_rooted"), sem("dve1")
        turned_done, turned_read = sem("h_turned"), sem("h_turned_read")
        vec_in, taps_in, blocks_in = sem("vec_in"), sem("taps_in"), sem("blocks_in")
        zeroed = sem("blocks_zeroed")
        product_done, product_read = sem("product_done"), sem("product_read")

        with nc.Block() as block:
            @block.sync
            def _(sp):
                for b in range(NT):
                    sp.dma_start(x_rows[:, b, :], d.x[b * P:(b + 1) * P, :]).then_inc(x_in[b], 16)
                    if b == 0:
                        sp.dma_start(gain[:], d.norm1_g.partition_broadcast(P)).then_inc(gain_in, 16)
                for g in range(2):
                    sp.dma_start(w[:, g], d.w_in[:, g * G:(g + 1) * G].rearrange("(k p) n -> p k n", p=P)
                                 ).then_inc(w_in[g], 16)
                for n in range(2):
                    load_qkv_weights(sp, d, m, n)

            @block.gpsimd
            def _(pool):
                pool.dma_start(wf[:], d.w_in[:, 5 * G:].rearrange("(k p) n -> p k n", p=P)).then_inc(small_in, 16)
                pool.wait_ge(small_in, 16)
                pool.dma_start(fbias[:], d.fox_bf.rearrange("(a b) -> a b", b=1)).then_inc(small_in, 16)
                pool.memset(m.wa[:], 0.0).then_inc(zeroed, 1)
                pool.memset(m.wx[:], 0.0).then_inc(zeroed, 1)
                for n, a in enumerate([d.conv_b, d.lru_ba, d.lru_bx, d.lru_lambda, d.gn_lru_g]):
                    if n:
                        pool.wait_ge(vec_in, 16 * n)
                    pool.dma_start(m.lru_vec[:, n], a.rearrange("(c p) -> p c", p=P),
                                   allow_slow_non_contiguous=True).then_inc(vec_in, 16)
                for j in range(d.TAPS):
                    if j:
                        pool.wait_ge(taps_in, 16 * j)
                    pool.dma_start(m.taps[:, :, j], d.conv_w[j].rearrange("(c p) -> p c", p=P),
                                   allow_slow_non_contiguous=True).then_inc(taps_in, 16)
                pool.wait_ge(zeroed, 2)
                n = 0
                for to, src in ((m.wa, d.lru_wa), (m.wx, d.lru_wx)):
                    for o in range(P // HD):
                        part = slice(o * HD, (o + 1) * HD)
                        if n:
                            pool.wait_ge(blocks_in, 16 * n)
                        pool.dma_start(to[part, :, part], src.rearrange("(c o) i j -> o i c j", o=P // HD)[o]
                                       ).then_inc(blocks_in, 16)
                        n += 1
                pool.wait_ge(vec_in, 80)
                pool.wait_ge(taps_in, 16 * d.TAPS)
                pool.wait_ge(blocks_in, 16 * n)

            @block.scalar
            def _(act):
                for b in range(NT):
                    act.wait_ge(x_in[b], 16)
                    if b:
                        act.wait_ge(summed, b)
                    nc.scalar.activation(squares[:], x_rows[:, b, :], ACT.Square,
                                         accum_out=sums[:, b:b + 1]).then_inc(summed, 1)
                act.wait_ge(dve1, 2)
                nc.scalar.activation(sums[:], sums[:], ACT.Sqrt).then_inc(rooted, 1)
                for b in range(NT):
                    act.wait_ge(turned_done, b + 1)
                    nc.scalar.activation(hT[:, :, b * P:(b + 1) * P], turned[:, b % 2], ACT.Copy
                                         ).then_inc(turned_read, 1)

                n = 0
                for g, (to, func) in enumerate([(m.xrT, ACT.Copy), (m.gateT, ACT.Gelu_apprx_tanh)]):
                    pad = d.PAD if g == 0 else 0
                    for c in range(CT):
                        for cols in halves(S // HALF):
                            act.wait_ge(product_done, n + 1)
                            nc.scalar.activation(to[:, c, pad + cols.start:pad + cols.stop], product[:, n % 4],
                                                 func).then_inc(product_read, 1)
                            n += 1
                act.wait_ge(small_in, 32)
                for cols in halves(S // HALF):
                    act.wait_ge(product_done, n + 1)
                    nc.scalar.activation(m.forget[:, cols], product[0:d.FH, n % 4], ACT.Identity,
                                         bias=fbias[:]).then_inc(product_read, 1)
                    n += 1

            @block.vector
            def _(dve):
                v = nc.vector
                own = Done(dve, dve1)
                own.mark(v.memset(m.xrT[:, :, 0:d.PAD], 0.0))
                dve.wait_ge(summed, NT)
                own.link(v.tensor_scalar(sums[:], sums[:], 1.0 / D, EPS, ALU.mult, ALU.add))
                dve.wait_ge(rooted, 1)
                own.link(v.reciprocal(rstd[:], sums[:]))
                dve.wait_ge(gain_in, 16)
                for b in range(NT):
                    if b >= 2:
                        dve.wait_ge(turned_done, b - 1)
                    own.mark(v.scalar_tensor_tensor(out=h_rows[:, b % 2], in0=x_rows[:, b, :], scalar=rstd[:, b:b + 1],
                                                    in1=gain[:], op0=ALU.mult, op1=ALU.mult))

            @block.tensor
            def _(pe):
                pe.wait_ge(m.ident_ready, 2)
                for b in range(NT):
                    pe.wait_ge(dve1, 4 + b)
                    if b >= 2:
                        pe.wait_ge(turned_read, b - 1)
                    for k in range(KT):
                        last = nc.tensor.transpose(turned[:, b % 2, k], h_rows[:, b % 2, k * P:(k + 1) * P], m.ident[:])
                    last.then_inc(turned_done, 1)
                pe.wait_ge(turned_read, NT)
                n = 0

                def product_bank():
                    if n >= 4:
                        pe.wait_ge(product_read, n - 3)

                for g in range(2):
                    pe.wait_ge(w_in[g], 16)
                    for c in range(CT):
                        for cols in halves(S // HALF):
                            product_bank()
                            for k in range(KT):
                                last = nc.tensor.matmul(product[:, n % 4], w[:, g, k, c * P:(c + 1) * P],
                                                        hT[:, k, cols], start=k == 0, stop=k == KT - 1)
                            last.then_inc(product_done, 1)
                            n += 1
                pe.wait_ge(small_in, 32)
                for cols in halves(S // HALF):
                    product_bank()
                    for k in range(KT):
                        last = nc.tensor.matmul(product[0:d.FH, n % 4], wf[:, k, :], hT[:, k, cols],
                                                start=k == 0, stop=k == KT - 1)
                    last.then_inc(product_done, 1)
                    n += 1


def load_qkv_weights(sp, d, m, n):
    width = d.GROUP // 2
    first = 2 * d.GROUP + n * width
    sp.dma_start(m.w_qkv[:, n % 2], d.w_in[:, first:first + width].rearrange("(k p) n -> p k n", p=P)
                 ).then_inc(m.w_qkv_in[n % 2], 16)


def recur(nc, d, m, sem):
    S, CT, NT, KT = d.S, d.GROUP // P, d.S // P, d.D // P
    WIDTH = d.GROUP // 2
    BANKS = 3
    products = [(wn, c, cols) for wn in range(4) for c in range(2) for cols in halves(2)]
    products += [(wn, None, slice(b * P, (b + 1) * P)) for wn in (4, 5) for b in range(NT)]
    last_with = [max(n for n, p in enumerate(products) if p[0] == wn) + 1 for wn in range(6)]
    with ExitStack() as own_memory:
        sb = lambda n, s, t=F32: own_memory.enter_context(nc.sbuf_tensor(n, s, t))
        ps = lambda n, s: own_memory.enter_context(nc.psum_tensor(n, s, F32))
        wa, wx, taps, vec = m.wa, m.wx, m.taps, m.lru_vec
        xc = sb("x_conv", [P, CT, S])
        r = sb("r_gate", [P, CT, S])
        ig = sb("i_gate", [P, CT, S])
        tanh = sb("tanh_m", [P, CT, S])
        tmp = sb("lru_tmp", [P, S])
        sp_e, sp_s, sp_q, sp_a = (sb(f"softplus_{n}", [P, CT]) for n in "esqa")
        decay = sb("decay", [P, CT])
        ndecay = sb("minus_decay", [P, CT])
        fe, fs, fq, fa = (xc[0:d.FH, c, :] for c in range(4))
        ones = tmp[0:d.FH, :]
        gates = ps("gates", [P, 2, 2, HALF])
        product = ps("product2", [P, BANKS, HALF])
        ssq = ps("ssq_lru", [P, HALF])

        dve2, act2 = sem("dve2"), sem("act2")
        gate_made, gate_read, ssq_done = sem("gate_made"), sem("gate_read"), sem("ssq_done")
        product_done, product_read = sem("product2_done"), sem("product2_read")
        EXP_LAMBDA = 2
        tanh_done = lambda c: EXP_LAMBDA + 2 * c + 1
        decay_exp_done = lambda c: EXP_LAMBDA + 2 * c + 2
        root_done = lambda c: EXP_LAMBDA + 2 * CT + c + 1
        square_done = lambda c: EXP_LAMBDA + 3 * CT + c + 1
        EXP_FORGET = EXP_LAMBDA + 4 * CT + 2
        conv_done = lambda c: d.TAPS * (c + 1)
        SOFTPLUS = conv_done(CT - 1) + 5 + LOG1P_TERMS - 2 + 2 + 4
        fraction_done = lambda c: SOFTPLUS + 3 * (c + 1)
        lru_done = lambda c: SOFTPLUS + 3 * CT + 4 * (c + 1)

        with nc.Block() as block:
            @block.sync
            def _(sp):
                for n in range(2, 6):
                    sp.wait_ge(product_done, last_with[n - 2])
                    load_qkv_weights(sp, d, m, n)

            @block.tensor
            def _(pe):
                def make(n):
                    wn, c, cols = products[n]
                    if n == 0 or products[n - 1][0] != wn:
                        pe.wait_ge(m.w_qkv_in[wn % 2], 16 * (wn // 2 + 1))
                    if n >= BANKS:
                        pe.wait_ge(product_read, n - BANKS + 1)
                    for k in range(KT):
                        if c is None:
                            last = nc.tensor.matmul(product[:, n % BANKS, 0:WIDTH], m.hT[:, k, cols],
                                                    m.w_qkv[:, wn % 2, k], start=k == 0, stop=k == KT - 1)
                        else:
                            last = nc.tensor.matmul(product[:, n % BANKS], m.w_qkv[:, wn % 2, k, c * P:(c + 1) * P],
                                                    m.hT[:, k, cols], start=k == 0, stop=k == KT - 1)
                    last.then_inc(product_done, 1)

                def gates_of(c):
                    pe.wait_ge(dve2, conv_done(c))
                    for n, w in ((2 * c, wa), (2 * c + 1, wx)):
                        if n >= 2:
                            pe.wait_ge(gate_read, n - 1)
                        for half, cols in enumerate(halves(2)):
                            last = nc.tensor.matmul(gates[:, n % 2, half], w[:, c, :], xc[:, c, cols],
                                                    start=True, stop=True)
                        last.then_inc(gate_made, 1)

                make(0)
                gates_of(0)
                make(1)
                gates_of(1)
                make(2)
                gates_of(2)
                gates_of(3)
                for n in range(3, len(products)):
                    make(n)
                pe.wait_ge(act2, square_done(CT - 1))
                for b in range(NT):
                    for c in range(CT):
                        last = nc.tensor.matmul(ssq[:, b:b + 1], r[:, c, b * P:(b + 1) * P], m.ones_col[:],
                                                start=c == 0, stop=c == CT - 1)
                last.then_inc(ssq_done, 1)

            @block.vector
            def _(dve):
                v = nc.vector
                own = Done(dve, dve2)
                for c in range(CT):
                    own.link(v.tensor_scalar(xc[:, c, :], m.xrT[:, c, 0:S], taps[:, c, 0:1], vec[:, 0, c:c + 1],
                                             ALU.mult, ALU.add))
                    for j in range(1, d.TAPS):
                        own.link(v.scalar_tensor_tensor(out=xc[:, c, :], in0=m.xrT[:, c, j:j + S],
                                                        scalar=taps[:, c, j:j + 1], in1=xc[:, c, :],
                                                        op0=ALU.mult, op1=ALU.add))
                dve.wait_ge(act2, EXP_LAMBDA)
                log1p_series(v, own, sp_e[:], sp_s[:], sp_q[:], sp_a[:])
                own.link(v.tensor_scalar(sp_s[:], vec[:, 3], -1.0, 0.0, ALU.mult, ALU.max))
                own.link(v.tensor_tensor(sp_a[:], sp_a[:], sp_s[:], ALU.add))
                own.link(v.tensor_scalar(decay[:], sp_a[:], LRU_C, None, ALU.mult))
                own.link(v.tensor_scalar(ndecay[:], sp_a[:], -LRU_C, None, ALU.mult))
                assert own.count == SOFTPLUS, own.count
                for c in range(CT):
                    dve.wait_ge(act2, tanh_done(c))
                    own.link(v.tensor_scalar(tmp[:], tanh[:, c, :], 1.0, None, ALU.add))
                    own.link(v.reciprocal(tmp[:], tmp[:]))
                    own.link(v.scalar_tensor_tensor(out=tanh[:, c, :], in0=tanh[:, c, :], scalar=2.0, in1=tmp[:],
                                                    op0=ALU.mult, op1=ALU.mult))
                for c in range(CT):
                    dve.wait_ge(act2, root_done(c))
                    own.link(v.tensor_tensor(xc[:, c, :], xc[:, c, :], ig[:, c, :], ALU.mult))
                    own.link(v.tensor_tensor(xc[:, c, :], xc[:, c, :], tanh[:, c, :], ALU.mult))
                    own.link(v.tensor_tensor_scan(out=ig[:, c, :], data0=r[:, c, :], data1=xc[:, c, :], initial=0.0,
                                                  op0=ALU.mult, op1=ALU.add))
                    own.link(v.tensor_tensor(m.gateT[:, c, :], m.gateT[:, c, :], ig[:, c, :], ALU.mult))
                    assert own.count == lru_done(c)
                for c in range(CT):
                    dve.wait_ge(act2, square_done(c))
                    own.link(v.tensor_scalar(m.gateT[:, c, :], m.gateT[:, c, :], vec[:, 4, c:c + 1], None, ALU.mult))
                dve.wait_ge(act2, EXP_FORGET)
                log1p_series(v, own, fe, fs, fq, fa)
                own.link(v.tensor_scalar(fs, m.forget[:], 0.0, None, ALU.min))
                own.link(v.tensor_tensor(fs, fs, fa, ALU.subtract))
                own.link(v.memset(ones, 1.0))
                own.link(v.tensor_tensor_scan(out=m.forget[:], data0=ones, data1=fs, initial=0.0,
                                              op0=ALU.mult, op1=ALU.add))
                dve.wait_ge(ssq_done, 1)
                own.link(v.tensor_scalar(m.rstd_lru[:], ssq[:, 0:S // P], 1.0 / d.GROUP, EPS, ALU.mult, ALU.add))

            @block.scalar
            def _(act):
                own = Done(act, act2)
                A = nc.scalar.activation

                def read(first, stop):
                    for n in range(first, stop):
                        wn, c, cols = products[n]
                        act.wait_ge(product_done, n + 1)
                        if c is None:
                            A(m.v[:, cols.start // P, (wn - 4) * WIDTH:(wn - 3) * WIDTH],
                              product[:, n % BANKS, 0:WIDTH], ACT.Copy).then_inc(product_read, 1)
                        else:
                            A(m.qk[:, wn // 2, wn % 2 * 2 + c, cols], product[:, n % BANKS], ACT.Copy,
                              scale=-d.QSCALE if wn < 2 else 1.0).then_inc(product_read, 1)

                def sigmoids(c):
                    for n, (to, bias) in ((2 * c, (r, 1)), (2 * c + 1, (ig, 2))):
                        act.wait_ge(gate_made, n + 1)
                        A(to[:, c, :], gates[:, n % 2].rearrange("p a b -> p (a b)"), ACT.Sigmoid,
                          bias=vec[:, bias, c:c + 1]).then_inc(gate_read, 1)

                own.link(A(sp_e[:], vec[:, 3], ACT.Abs))
                own.link(A(sp_e[:], sp_e[:], ACT.Exp, scale=-1.0))
                read(0, 1)
                sigmoids(0)
                read(1, 2)
                sigmoids(1)
                read(2, 3)
                sigmoids(2)
                sigmoids(3)
                act.wait_ge(dve2, SOFTPLUS)
                for c in range(CT):
                    act.wait_ge(gate_read, 2 * c + 1)
                    own.mark(A(tanh[:, c, :], r[:, c, :], ACT.Tanh, scale=decay[:, c:c + 1]))
                    own.wait(own.count)
                    own.mark(A(r[:, c, :], r[:, c, :], ACT.Exp, scale=ndecay[:, c:c + 1]))
                read(3, 5)
                for c in range(CT):
                    act.wait_ge(dve2, fraction_done(c))
                    own.mark(A(tanh[:, c, :], tanh[:, c, :], ACT.Sqrt))
                    assert own.count == root_done(c)
                    read(5 + c, 6 + c)
                for c in range(CT):
                    act.wait_ge(dve2, lru_done(c))
                    own.mark(A(r[:, c, :], m.gateT[:, c, :], ACT.Square))
                    read(9 + c, 10 + c)
                own.link(A(fe, m.forget[:], ACT.Abs))
                own.link(A(fe, fe, ACT.Exp, scale=-1.0))
                assert own.count == EXP_FORGET
                read(13, len(products))


def attend(nc, d, m, sem):
    S, NT, HD, FH = d.S, d.S // P, d.FHD, d.FH
    IN_PAIR = 2 * NT
    ITEMS = 2 * IN_PAIR
    PASSES = FH // 4
    parts_of = [(n % NT + 4) // 4 for n in range(ITEMS)]
    parts_to = [sum(parts_of[:n]) for n in range(ITEMS + 1)]
    lows_to = [sum(1 for k in range(n) if k % NT) for n in range(ITEMS + 1)]
    with ExitStack() as own_memory:
        sb = lambda n, s, t=F32: own_memory.enter_context(nc.sbuf_tensor(n, s, t))
        ps = lambda n, s: own_memory.enter_context(nc.psum_tensor(n, s, F32))
        pick = sb("pick_head", [FH, FH, P])
        later = sb("later_keys", [P, P])
        Fb = sb("forget_sums", [P, FH, S])
        Fp = sb("forget_sums_pair", [P, 2, 2, S])
        Fm = sb("forget_sums_masked", [P, 2, P])
        qp, kp = sb("q_pair", [P, 2, S]), sb("k_pair", [P, 2, S])
        vp = sb("v_pair", [P, 2, NT, P])
        neg = sb("neg_logits", [P, 2, S])
        low = sb("lowest", [P, 2, 2])
        prob = sb("probs", [P, 2, S])
        total = sb("totals", [P, 2])
        inv = sb("inv_totals", [P, 2])
        probT = sb("probs_turned", [P, 2, S])
        logit = ps("logits", [P, 2, 2, HALF])
        turned = ps("probs_turned_ps", [P, 2, 4, P])
        mixed = ps("mixed_values", [P, 2, HALF])

        low_done, fb_read, pair_in = sem("low_done"), sem("sums_spread"), sem("pair_copied")
        pool_apart = sem("attend_pool_waits")
        apart = sem("attend_waits")
        logits_done, logits_read = sem("logits_done"), sem("logits_read")
        probs_done = sem("probs_done")
        part_turned, part_read = sem("part_turned"), sem("part_read")
        mixed_done, mixed_read = sem("mixed_done"), sem("mixed_read")
        inv_done, picked = sem("inv_done"), sem("picked")
        fb_done, fp_done, fm_done = sem("fb_done"), sem("fp_done"), sem("fm_done")

        with nc.Block() as block:
            @block.gpsimd
            def _(pool):
                pool.memset(pick[:], 0.0).then_inc(picked, 1)
                pool.wait_ge(picked, 1)
                pool.affine_select(out=pick[:], in_=pick[:], compare_op=ALU.not_equal, fill=1.0, base=0,
                                   pattern=[[-1, FH], [0, P]], channel_multiplier=1).then_inc(picked, 1)
                pool.memset(later[:], 0.0).then_inc(picked, 1)
                pool.wait_ge(picked, 3)
                pool.affine_select(out=later[:], in_=later[:], compare_op=ALU.is_ge, fill=BIG, base=0,
                                   pattern=[[-1, P]], channel_multiplier=1).then_inc(picked, 1)
                with pool.Fori(0, PASSES) as i:
                    for b in range(2):
                        pool.wait_ge(mixed_done, i * ITEMS + b * IN_PAIR + 1)
                        pool.sem_inc(pool_apart, 1)
                        pool.tensor_copy(qp[:, b], m.qT[:, bass.ds(2 * i + b, 1), :].rearrange("p a s -> p (a s)")
                                         ).then_inc(pair_in, 1)
                        pool.tensor_copy(kp[:, b], m.kT[:, bass.ds(2 * i + b, 1), :].rearrange("p a s -> p (a s)")
                                         ).then_inc(pair_in, 1)
                        pool.tensor_copy(vp[:, b], m.v[:, :, bass.ds((2 * i + b) * P, P)]).then_inc(pair_in, 1)

            @block.tensor
            def _(pe):
                pe.wait_ge(picked, 4)
                pe.sem_inc(mixed_done, IN_PAIR + 1)
                for h in range(FH):
                    if h >= 2:
                        pe.wait_ge(fb_read, h - 1)
                    for half, cols in enumerate(halves(2)):
                        last = nc.tensor.matmul(logit[:, h % 2, half], pick[:, h, :], m.forget[:, cols],
                                                start=True, stop=True)
                    last.then_inc(fb_done, 1)
                pe.wait_ge(fb_read, FH)

                def scores(i, n):
                    b, h, qt = n // IN_PAIR, n // NT % 2, n % NT
                    part = slice(h * HD, (h + 1) * HD)
                    if n % IN_PAIR == 0:
                        pe.wait_ge(pair_in, i * 6 + 3 * (b + 1))
                    pe.wait_ge(logits_read, i * ITEMS + n + 1)
                    for half in range(qt // 4 + 1):
                        width = min(HALF, (qt + 1) * P - half * HALF)
                        last = nc.tensor.matmul(logit[:, n % 2, half, 0:width], qp[part, b, qt * P:(qt + 1) * P],
                                                kp[part, b, half * HALF:half * HALF + width], start=True, stop=True)
                    last.then_inc(logits_done, 1)

                def turn(i, n):
                    qt = n % NT
                    pe.wait_ge(probs_done, i * ITEMS + n + 1)
                    for g in range(parts_of[n]):
                        at = parts_to[n] + g
                        pe.wait_ge(part_read, i * parts_to[ITEMS] + at + 1)
                        for kb in range(4 * g, min(4 * g + 4, qt + 1)):
                            last = nc.tensor.transpose(turned[:, at % 2, kb - 4 * g],
                                                       prob[:, n % 2, kb * P:(kb + 1) * P], m.ident[:])
                        last.then_inc(part_turned, 1)

                def weigh(i, n):
                    b, h, qt = n // IN_PAIR, n // NT % 2, n % NT
                    pe.wait_ge(part_read, i * parts_to[ITEMS] + parts_to[n + 1] + 2)
                    pe.wait_ge(mixed_read, i * ITEMS + n + 1)
                    for kb in range(qt + 1):
                        last = nc.tensor.matmul(mixed[:, n % 2, 0:HD], probT[:, n % 2, kb * P:(kb + 1) * P],
                                                vp[:, b, kb, h * HD:(h + 1) * HD], start=kb == 0, stop=kb == qt)
                    last.then_inc(mixed_done, 1)

                with pe.Fori(0, PASSES) as i:
                    scores(i, 0)
                    scores(i, 1)
                    for n in range(ITEMS):
                        turn(i, n)
                        if n:
                            weigh(i, n - 1)
                        if n + 2 < ITEMS:
                            scores(i, n + 2)
                    weigh(i, ITEMS - 1)

            @block.scalar
            def _(act):
                act.sem_inc(part_read, 2)
                for h in range(FH):
                    act.wait_ge(fb_done, h + 1)
                    nc.scalar.activation(Fb[:, h, :], logit[:, h % 2].rearrange("p a b -> p (a b)"), ACT.Copy
                                         ).then_inc(fb_read, 1)
                act.wait_ge(fb_read, FH)

                def sums(i, b):
                    act.wait_ge(logits_read, i * ITEMS + 2)
                    nc.scalar.activation(Fp[:, b], Fb[:, bass.ds(4 * i + 2 * b, 2), :], ACT.Copy).then_inc(fp_done, 1)

                def exps(i, n):
                    W = (n % NT + 1) * P
                    act.wait_ge(logits_read, i * ITEMS + n + 3)
                    if n >= 2:
                        act.wait_ge(part_turned, i * parts_to[ITEMS] + parts_to[n - 1])
                        act.wait_ge(inv_done, i * ITEMS + n - 1)
                    nc.scalar.activation(prob[:, n % 2, 0:W], neg[:, n % 2, 0:W], ACT.Exp, scale=-1.0,
                                         bias=low[:, n % 2, 1:2], accum_out=total[:, n % 2:n % 2 + 1]
                                         ).then_inc(probs_done, 1)

                def copies(i, n):
                    if n >= 2:
                        act.wait_ge(mixed_done, i * ITEMS + n + IN_PAIR)
                    for g in range(parts_of[n]):
                        k = min(4, n % NT + 1 - 4 * g)
                        at = parts_to[n] + g
                        act.wait_ge(part_turned, i * parts_to[ITEMS] + at + 1)
                        nc.scalar.activation(probT[:, n % 2, 4 * g * P:(4 * g + k) * P],
                                             turned[:, at % 2, 0:k].rearrange("p a b -> p (a b)"),
                                             ACT.Copy).then_inc(part_read, 1)

                with act.Fori(0, PASSES) as i:
                    sums(i, 0)
                    sums(i, 1)
                    exps(i, 0)
                    for n in range(ITEMS):
                        if n + 1 < ITEMS:
                            exps(i, n + 1)
                        copies(i, n)

            @block.vector
            def _(dve):
                v = nc.vector
                dve.wait_ge(picked, 4)
                dve.sem_inc(logits_read, 2)
                dve.sem_inc(mixed_read, 2)

                def finish(i, n):
                    b, h, qt = n // IN_PAIR, n // NT % 2, n % NT
                    dve.wait_ge(probs_done, i * ITEMS + n + 1)
                    v.reciprocal(inv[:, n % 2:n % 2 + 1], total[:, n % 2:n % 2 + 1]).then_inc(inv_done, 1)
                    dve.wait_ge(inv_done, i * ITEMS + n + 1)
                    dve.wait_ge(mixed_done, i * ITEMS + n + 2 + IN_PAIR)
                    v.tensor_scalar(m.fox[:, qt, bass.ds((2 * i + b) * P + h * HD, HD)], mixed[:, n % 2, 0:HD],
                                    inv[:, n % 2:n % 2 + 1], None, ALU.mult).then_inc(mixed_read, 1)

                def logits(i, n):
                    b, h, qt = n // IN_PAIR, n // NT % 2, n % NT
                    own_block = slice(qt * P, (qt + 1) * P)
                    if n % IN_PAIR == 0:
                        dve.wait_ge(fp_done, 2 * i + b + 1)
                    v.tensor_tensor(Fm[:, n % 2], Fp[:, b, h, own_block], later[:], ALU.add).then_inc(fm_done, 1)
                    dve.wait_ge(logits_done, i * ITEMS + n + 1)
                    if n >= 2:
                        dve.wait_ge(probs_done, i * ITEMS + n - 1)
                    dve.sem_inc(apart, 1)
                    src = logit[:, n % 2].rearrange("p a b -> p (a b)")
                    least = 3.0e38
                    if qt:
                        least = low[:, n % 2, 0:1]
                        v.tensor_tensor_reduce(out=neg[:, n % 2, 0:qt * P], in0=src[:, 0:qt * P],
                                               in1=Fp[:, b, h, 0:qt * P], scale=1.0, scalar=3.0e38, op0=ALU.add,
                                               op1=ALU.min, accum_out=low[:, n % 2, 0:1]).then_inc(low_done, 1)
                        dve.wait_ge(low_done, i * lows_to[ITEMS] + lows_to[n + 1])
                    dve.wait_ge(fm_done, i * ITEMS + n + 1)
                    dve.sem_inc(apart, 1)
                    v.tensor_tensor_reduce(out=neg[:, n % 2, own_block], in0=src[:, own_block], in1=Fm[:, n % 2],
                                           scale=1.0, scalar=least, op0=ALU.add, op1=ALU.min,
                                           accum_out=low[:, n % 2, 1:2]).then_inc(logits_read, 1)

                with dve.Fori(0, PASSES) as i:
                    logits(i, 0)
                    logits(i, 1)
                    for n in range(ITEMS):
                        if n:
                            finish(i, n - 1)
                        if n + 2 < ITEMS:
                            logits(i, n + 2)
                    finish(i, ITEMS - 1)


def mix_out(nc, d, m, sem):
    D, S, G = d.D, d.S, d.GROUP
    NT, CT, KT = S // P, G // P, D // P
    with ExitStack() as own_memory:
        sb = lambda n, s, t=F32: own_memory.enter_context(nc.sbuf_tensor(n, s, t))
        ps = lambda n, s: own_memory.enter_context(nc.psum_tensor(n, s, F32))
        w = sb("w_out_sb", [P, 2 * CT, D])
        x_row = sb("x_row", [P, 2, D])
        x2 = sb("x2_row", [P, 2, D])
        gain_fox, gain2 = sb("gain_fox", [P, G]), sb("gain2", [P, D])
        fox_rows = sb("fox_rows", [P, 2, G])
        foxT = sb("foxT", [P, CT, S])
        squares_fox, squares = sb("squares_fox", [P, G]), sb("squares4", [P, D])
        h2_rows = sb("h2_rows", [P, 2, D])
        ssq_fox, ssq = sb("ssq_fox", [P, NT]), sb("ssq4", [P, NT])
        rfox, r2 = sb("rstd_fox", [P, NT]), sb("rstd2", [P, NT])
        turned_fox = ps("turned_fox", [P, 2, CT, P])
        out_lru = ps("out_lru", [P, 2, HALF])
        out_fox = ps("out_fox", [P, 2, HALF])
        turned = ps("turned_h2", [P, KT, P])

        w_in, gains_in = sem("w_out_in"), sem("gains_in")
        x_in = [sem("x_row_in0"), sem("x_row_in1")]
        x2_stored = [sem("x2_stored0"), sem("x2_stored1")]
        fox_sum, fox_root, dve4 = sem("fox_sum"), sem("fox_root"), sem("dve4")
        fox_turned, foxT_done = sem("fox_turned"), sem("foxT_done")
        mixed, squared, rooted = sem("out_mixed"), sem("x2_squared"), sem("x2_rooted")
        h2_turned, h2_hi = sem("h2_turned"), sem("h2_hi")
        BEFORE, LRU_READ, X2, VAR, ROWS, TILE = 3 + NT, 1, 2, 3, 5, 6

        with nc.Block() as block:
            @block.sync
            def _(sp):
                sp.dma_start(gain_fox[:], d.gn_fox_g.partition_broadcast(P)).then_inc(gains_in, 16)
                sp.wait_ge(gains_in, 16)
                sp.dma_start(gain2[:], d.norm2_g.partition_broadcast(P)).then_inc(gains_in, 16)
                sp.dma_start(w[:], d.w_out.rearrange("(k p) n -> p k n", p=P)).then_inc(w_in, 16)
                for b in range(NT):
                    if b >= 2:
                        sp.wait_ge(dve4, BEFORE + TILE * (b - 2) + X2)
                    sp.dma_start(x_row[:, b % 2], d.x[b * P:(b + 1) * P, :]).then_inc(x_in[b % 2], 16)
                    if b >= 2:
                        sp.dma_start(d.x2[(b - 2) * P:(b - 1) * P, :], x2[:, b % 2]).then_inc(x2_stored[b % 2], 16)
                for b in (NT - 2, NT - 1):
                    sp.wait_ge(dve4, BEFORE + TILE * b + X2)
                    sp.dma_start(d.x2[b * P:(b + 1) * P, :], x2[:, b % 2]).then_inc(x2_stored[b % 2], 16)
                sp.wait_ge(x2_stored[0], 16 * NT // 2)
                sp.wait_ge(x2_stored[1], 16 * NT // 2)

            @block.scalar
            def _(act):
                A = nc.scalar.activation
                for b in range(NT):
                    if b:
                        act.wait_ge(fox_sum, b)
                    A(squares_fox[:], m.fox[:, b, :], ACT.Square, accum_out=ssq_fox[:, b:b + 1]).then_inc(fox_sum, 1)
                act.wait_ge(dve4, 1)
                A(m.rstd_lru[:], m.rstd_lru[:], ACT.Sqrt).then_inc(fox_root, 1)
                A(ssq_fox[:], ssq_fox[:], ACT.Sqrt).then_inc(fox_root, 1)
                for b in range(NT):
                    act.wait_ge(fox_turned, b + 1)
                    A(foxT[:, :, b * P:(b + 1) * P], turned_fox[:, b % 2], ACT.Copy).then_inc(foxT_done, 1)
                for b in range(NT):
                    act.wait_ge(dve4, BEFORE + TILE * b + X2)
                    if b:
                        act.wait_ge(squared, b)
                    A(squares[:], x2[:, b % 2], ACT.Square, accum_out=ssq[:, b:b + 1]).then_inc(squared, 1)
                    act.wait_ge(dve4, BEFORE + TILE * b + VAR)
                    A(r2[:, b:b + 1], r2[:, b:b + 1], ACT.Sqrt).then_inc(rooted, 1)
                    act.wait_ge(h2_turned, b + 1)
                    A(m.h2T[:, 0, :, b * P:(b + 1) * P], turned[:], ACT.Copy).then_inc(h2_hi, 1)

            @block.vector
            def _(dve):
                v = nc.vector
                own = Done(dve, dve4)
                dve.wait_ge(fox_sum, NT)
                own.link(v.tensor_scalar(ssq_fox[:], ssq_fox[:], 1.0 / G, EPS, ALU.mult, ALU.add))
                dve.wait_ge(fox_root, 2)
                own.mark(v.reciprocal(m.rstd_lru[:], m.rstd_lru[:]))
                own.link(v.reciprocal(rfox[:], ssq_fox[:]))
                dve.wait_ge(gains_in, 32)
                for b in range(NT):
                    if b >= 2:
                        dve.wait_ge(fox_turned, b - 1)
                    own.mark(v.scalar_tensor_tensor(out=fox_rows[:, b % 2], in0=m.fox[:, b, :],
                                                    scalar=rfox[:, b:b + 1], in1=gain_fox[:],
                                                    op0=ALU.mult, op1=ALU.mult))
                for b in range(NT):
                    s = b % 2
                    dve.wait_ge(mixed, b + 1)
                    dve.wait_ge(x_in[s], 16 * (b // 2 + 1))
                    if b >= 2:
                        dve.wait_ge(x2_stored[s], 16 * (b // 2))
                    own.link(v.scalar_tensor_tensor(out=x2[:, s], in0=out_lru[:].rearrange("p a b -> p (a b)"),
                                                    scalar=m.rstd_lru[:, b:b + 1], in1=x_row[:, s],
                                                    op0=ALU.mult, op1=ALU.add))
                    own.link(v.tensor_tensor(x2[:, s], x2[:, s], out_fox[:].rearrange("p a b -> p (a b)"), ALU.add))
                    dve.wait_ge(squared, b + 1)
                    own.mark(v.tensor_scalar(r2[:, b:b + 1], ssq[:, b:b + 1], 1.0 / D, EPS, ALU.mult, ALU.add))
                    dve.wait_ge(rooted, b + 1)
                    own.link(v.reciprocal(r2[:, b:b + 1], r2[:, b:b + 1]))
                    own.link(v.scalar_tensor_tensor(out=h2_rows[:, s], in0=x2[:, s], scalar=r2[:, b:b + 1],
                                                    in1=gain2[:], op0=ALU.mult, op1=ALU.mult))
                    dve.wait_ge(h2_hi, b + 1)
                    own.link(v.tensor_tensor(m.h2T[:, 1, :, b * P:(b + 1) * P], turned[:],
                                             m.h2T[:, 0, :, b * P:(b + 1) * P].bitcast(F32), ALU.subtract))
                assert own.count == BEFORE + TILE * NT

            @block.tensor
            def _(pe):
                for b in range(NT):
                    pe.wait_ge(dve4, 3 + b + 1)
                    if b >= 2:
                        pe.wait_ge(foxT_done, b - 1)
                    for c in range(CT):
                        last = nc.tensor.transpose(turned_fox[:, b % 2, c], fox_rows[:, b % 2, c * P:(c + 1) * P],
                                                   m.ident[:])
                    last.then_inc(fox_turned, 1)
                pe.wait_ge(w_in, 16)
                pe.wait_ge(foxT_done, NT)

                def turn(b):
                    pe.wait_ge(dve4, BEFORE + TILE * b + ROWS)
                    for k in range(KT):
                        last = nc.tensor.transpose(turned[:, k], h2_rows[:, b % 2, k * P:(k + 1) * P], m.ident[:])
                    last.then_inc(h2_turned, 1)

                for b in range(NT):
                    for to, of, first, step in ((out_lru, m.gateT, 0, LRU_READ), (out_fox, foxT, CT, X2)):
                        if b:
                            pe.wait_ge(dve4, BEFORE + TILE * (b - 1) + step)
                        for half, cols in enumerate(halves(2)):
                            for c in range(CT):
                                last = nc.tensor.matmul(to[:, half], of[:, c, b * P:(b + 1) * P], w[:, first + c, cols],
                                                        start=c == 0, stop=c == CT - 1)
                    last.then_inc(mixed, 1)
                    if b:
                        turn(b - 1)
                turn(NT - 1)


def score(nc, d, m, sem):
    D, S, NK = d.D, d.S, d.NK
    KT, NT, HP = D // P, S // P, 2 * d.PH
    with ExitStack() as own_memory:
        sb = lambda n, s, t=F32: own_memory.enter_context(nc.sbuf_tensor(n, s, t))
        ps = lambda n, s: own_memory.enter_context(nc.psum_tensor(n, s, F32))
        keys = sb("subkey_rows", [P, HP, P])
        keysT = sb("subkeysT", [P, HP, P])
        w = sb("wq_tile", [P, 2, KT, P])
        whi = sb("wq_hi", [P, 2, KT, P], F32R)
        wlo = sb("wq_lo", [P, 2, KT, P], F32R)
        qT = sb("peer_qT", [P, 2, S])
        rows = sb("score_rows", [P, 2, NT, NK])
        query = ps("query", [P, 2, HALF])
        score_ps = ps("score_ps", [P, 2, NT, NK])
        keys_ps = ps("keys_ps", [P, 4, P])

        keys_in = sem("keys_in")
        w_in = [sem("wq_in0"), sem("wq_in1")]
        stored = [sem("scores_stored0"), sem("scores_stored1")]
        keys_turned, keysT_done = sem("keys_turned"), sem("keysT_done")
        hi_done, lo_done = sem("wq_hi_done"), sem("wq_lo_done")
        query_done, query_read = sem("query_done"), sem("query_read")
        scored, scores_read, apart = sem("scored"), sem("scores_read"), sem("score_waits")

        with nc.Block() as block:
            @block.sync
            def _(sp):
                sp.dma_start(keys[:], d.peer_subkeys.rearrange("h n c -> n h c")).then_inc(keys_in, 16)
                with sp.Fori(0, HP // 2) as i:
                    for b in range(2):
                        sp.wait_ge(lo_done, 2 * i + 1)
                        sp.dma_start(w[:, b], d.peer_wq[:, bass.ds((2 * i + b) * P, P)]
                                     .rearrange("(k p) n -> p k n", p=P)).then_inc(w_in[b], 16)

            @block.gpsimd
            def _(pool):
                with pool.Fori(0, HP // 2) as i:
                    for b in range(2):
                        pool.wait_ge(w_in[b], 16 * (i + 1))
                        pool.wait_ge(query_done, (2 * i + b) * 2 + 1)
                        pool.sem_inc(apart, 1)
                        pool.tensor_copy(whi[:, b], w[:, b]).then_inc(hi_done, 1)

            @block.vector
            def _(dve):
                dve.sem_inc(lo_done, 1)
                with dve.Fori(0, HP // 2) as i:
                    for b in range(2):
                        dve.wait_ge(hi_done, 2 * i + b + 1)
                        nc.vector.tensor_tensor(wlo[:, b], w[:, b], whi[:, b].bitcast(F32), ALU.subtract
                                                ).then_inc(lo_done, 1)

            @block.tensor
            def _(pe):
                pe.wait_ge(keys_in, 16)
                for g in range(HP // 4):
                    if g:
                        pe.wait_ge(keysT_done, g)
                    for j in range(4):
                        last = nc.tensor.transpose(keys_ps[:, j], keys[:, 4 * g + j, :], m.ident[:])
                    last.then_inc(keys_turned, 1)
                pe.wait_ge(keysT_done, HP // 4)
                pe.sem_inc(query_done, 3)
                with pe.Fori(0, HP // 2) as i:
                    for b in range(2):
                        pe.wait_ge(lo_done, 2 * i + b + 2)
                        for half, cols in enumerate(halves(2)):
                            pe.wait_ge(query_read, (2 * i + b) * 2 + half + 1)
                            for n, (part, t) in enumerate([(whi, 0), (whi, 1), (wlo, 0)]):
                                for k in range(KT):
                                    last = nc.tensor.matmul(query[:, half], part[:, b, k], m.h2T[:, t, k, cols],
                                                            start=n == 0 and k == 0, stop=n == 2 and k == KT - 1)
                            last.then_inc(query_done, 1)
                        pe.wait_ge(query_read, (2 * i + b) * 2 + 4)
                        pe.wait_ge(scores_read, 2 * i + b + 1)
                        for t in range(NT):
                            last = nc.tensor.matmul(score_ps[:, b, t], qT[:, b, t * P:(t + 1) * P],
                                                    keysT[:, bass.ds(2 * i + b, 1), :].rearrange("p a n -> p (a n)"),
                                                    start=True, stop=True)
                        last.then_inc(scored, 1)

            @block.scalar
            def _(act):
                A = nc.scalar.activation
                for g in range(HP // 4):
                    act.wait_ge(keys_turned, g + 1)
                    A(keysT[:, 4 * g:4 * g + 4, :], keys_ps[:], ACT.Copy).then_inc(keysT_done, 1)
                act.sem_inc(query_read, 2)
                act.sem_inc(scores_read, 2)
                act.sem_inc(stored[0], 16)
                act.sem_inc(stored[1], 16)
                with act.Fori(0, HP // 2) as i:
                    for b in range(2):
                        for half, cols in enumerate(halves(2)):
                            act.wait_ge(query_done, (2 * i + b) * 2 + half + 4)
                            A(qT[:, b, cols], query[:, half], ACT.Copy).then_inc(query_read, 1)
                        act.wait_ge(scored, 2 * i + b + 1)
                        act.wait_ge(stored[b], 16 * i + 16)
                        A(rows[:, b], score_ps[:, b], ACT.Copy).then_inc(scores_read, 1)
                        act.wait_ge(scores_read, 2 * i + b + 3)
                        act.dma_start(d.scores[:, :, bass.ds(2 * i + b, 1), :].rearrange("t p a n -> p t (a n)"),
                                      rows[:, b]).then_inc(stored[b], 16)
                act.wait_ge(stored[0], 16 * (HP // 2) + 16)
                act.wait_ge(stored[1], 16 * (HP // 2) + 16)


def experts_up(nc, d, m, sem):
    D, S, NK, PH, TOP = d.D, d.S, d.NK, d.PH, d.TOP
    KT, NT = D // P, S // P
    FIRST, STEPS = 16, 14
    assert FIRST + NT * STEPS == NK and FIRST % 2 == 0 and STEPS % 2 == 0
    GROUP = 4
    GROUPS = P // GROUP
    SLOTS = 4
    u_rows = d.peer_u.rearrange("(p e) n -> p e n", p=NK)
    with ExitStack() as own_memory:
        sb = lambda n, s, t=F32: own_memory.enter_context(nc.sbuf_tensor(n, s, t))
        ps = lambda n, s: own_memory.enter_context(nc.psum_tensor(n, s, F32))
        u = sb("u_chunk", [P, 2, D])
        uhi = sb("uT_hi", [P, 2, KT, P], F32R)
        ulo = sb("uT_lo", [P, 2, KT, P], F32R)
        act_out = sb("expert_acts", [P, 2, S])
        first_hot = sb("first_hot", [P, SLOTS, GROUP, NK], F32R)
        second_hi = sb("second_hot_hi", [P, SLOTS, GROUP, NK], F32R)
        second_lo = sb("second_hot_lo", [P, SLOTS, GROUP, NK], F32R)
        spread = sb("gates_spread", [P, 2, NK, P // 2])
        sc = sb("scores_tile", [P, 2 * PH, NK])
        rest = sb("scores_rest", [P, 2, NK])
        val = sb("top_values", [P, PH, 2, TOP])
        idx = sb("top_indices", [P, PH, 2, TOP], U32)
        cand = sb("pair_scores", [P, TOP, TOP])
        crest = sb("pair_rest", [P, TOP * TOP])
        pval = sb("pair_values", [P, PH, TOP])
        pidx = sb("pair_indices", [P, PH, TOP], U32)
        pdig = sb("pair_digits", [P, 2, PH, TOP], U32)
        idxf = sb("top_indices_f", [P, PH, 2, TOP])
        pdigf = sb("pair_digits_f", [P, 2, PH, TOP])
        assert 2 * PH * NK == PH * TOP * TOP
        hot = sc[:].rearrange("p a b -> p (a b)").rearrange("p (k r) -> p k r", r=TOP)
        route = sb("route", [P, 3, PH, TOP])
        gsum = sb("gate_sums", [P, PH])
        routeT = sb("routeT", [P, 3, P])
        gate_hi, gate_lo = sb("gateT_hi", [P, P], F32R), sb("gateT_lo", [P, P])
        turned = ps("u_turned_ps", [P, KT, P])
        pre = ps("expert_pre", [P, 2, HALF])
        spread_ps = ps("spread_ps", [P, 2, GROUP, NK])
        route_ps = ps("route_ps", [P, 3, P])

        u_in = [sem("u_in0"), sem("u_in1")]
        sc_in, sc_used = sem("scores_tile_in"), sem("scores_tile_used")
        u_turned, hi_done, lo_done = sem("u_turned"), sem("u_hi_done"), sem("u_lo_done")
        pre_done, act_done = sem("pre_done"), sem("expert_act_done")
        act_stored = [sem("act_stored0"), sem("act_stored1")]
        gates_hot = sem("gates_hot")
        hot_done, spread_done, spread_read = sem("hot_done"), sem("spread_done"), sem("spread_read")
        spread_stored = [sem("spread_stored0"), sem("spread_stored1")]
        picked = sem("route_step")
        shifted, exp_done = sem("pairs_shifted"), sem("pairs_exp")
        route_done, route_turned, routeT_done = sem("route_done"), sem("route_turned"), sem("routeT_done")

        HEAD_STEPS = 16
        TILE_STEPS = PH * HEAD_STEPS + 12

        keys = m.iota[:].rearrange("p (a n) -> p a n", a=1).to_broadcast([P, GROUP, NK])
        each = lambda values: values.rearrange("p (t a) -> p t a", a=1).to_broadcast([P, GROUP, NK])

        def passes(engine, body):
            body(0, None, 0)
            with engine.Fori(0, NT - 1) as i:
                body(FIRST + STEPS * i, i, i + 1)
            body(FIRST + STEPS * (NT - 1), NT - 1, None)

        def groups_of(step):
            return range(step * GROUPS // STEPS, (step + 1) * GROUPS // STEPS)

        def spread_at(step, half):
            if half == 0:
                return list(groups_of(step - 1))[-1:] if step else []
            return list(groups_of(step))[:None if step == STEPS - 1 else -1]

        def steps_of(tile):
            return FIRST if tile is None else STEPS

        def slot_turns(chunk0, tile):
            if isinstance(chunk0, int):
                return chunk0 // 2
            return FIRST // 2 + (STEPS // 2) * tile

        with nc.Block() as block:
            @block.sync
            def _(sp):
                def body(c0, tile, select):
                    for s in range(steps_of(tile)):
                        if s == 1 and select is not None:
                            sp.wait_ge(sc_used, select)
                            sp.dma_start(sc[:], d.scores[bass.ds(select, 1)].rearrange("a p h n -> p (a h) n")
                                         ).then_inc(sc_in, 16)
                        sp.wait_ge(u_turned, c0 + s)
                        sp.dma_start(u[:, s % 2], u_rows[:, bass.ds(c0 + s, 1), :].rearrange("p a n -> p (a n)")
                                     ).then_inc(u_in[s % 2], 16)
                passes(sp, body)

            @block.tensor
            def _(pe):
                pe.sem_inc(u_turned, 1)
                pe.sem_inc(pre_done, 2)
                pe.sem_inc(spread_done, SLOTS)

                def turn(chunk, s, turns):
                    pe.wait_ge(u_in[s % 2], 16 * (turns + 1))
                    pe.wait_ge(lo_done, chunk)
                    for k in range(KT):
                        last = nc.tensor.transpose(turned[:, k], u[:, s % 2, k * P:(k + 1) * P], m.ident[:])
                    last.then_inc(u_turned, 1)

                def multiply(chunk, s, half, cols):
                    pe.wait_ge(act_done, 2 * chunk + half)
                    for n, (part, t) in enumerate([(uhi, 0), (uhi, 1), (ulo, 0)]):
                        for k in range(KT):
                            last = nc.tensor.matmul(pre[:, half], part[:, s % 2, k], m.h2T[:, t, k, cols],
                                                    start=n == 0 and k == 0, stop=n == 2 and k == KT - 1)
                    last.then_inc(pre_done, 1)

                def spread_group(tile, g):
                    pe.wait_ge(gates_hot, tile * GROUPS + g + 1)
                    pe.wait_ge(spread_read, tile * GROUPS + g + 1)
                    for j in range(GROUP):
                        nc.tensor.matmul(spread_ps[:, g % 2, j], first_hot[:, g % SLOTS, j],
                                         second_hi[:, g % SLOTS, j], start=True, stop=False)
                        last = nc.tensor.matmul(spread_ps[:, g % 2, j], first_hot[:, g % SLOTS, j],
                                                second_lo[:, g % SLOTS, j], start=False, stop=True)
                    last.then_inc(spread_done, 1)

                turn(0, 0, 0)

                def body(c0, tile, select):
                    turns, steps = slot_turns(c0, tile), steps_of(tile)
                    for s in range(steps):
                        if s + 1 < steps or select is not None:
                            turn(c0 + s + 1, s + 1, turns + (s + 1) // 2)
                        pe.wait_ge(lo_done, c0 + s + 1)
                        for half, cols in enumerate(halves()):
                            multiply(c0 + s, s, half, cols)
                            if tile is not None:
                                for g in spread_at(s, half):
                                    spread_group(tile, g)
                        if s == STEPS - 1 and select is not None:
                            pe.wait_ge(route_done, select + 1)
                            for n in range(3):
                                last = nc.tensor.transpose(route_ps[:, n], route[:, n].rearrange("p a b -> p (a b)"),
                                                           m.ident[:])
                            last.then_inc(route_turned, 1)
                passes(pe, body)

            @block.scalar
            def _(act):
                A = nc.scalar.activation
                act.sem_inc(act_done, 1)
                act.sem_inc(spread_read, 2)
                act.sem_inc(spread_stored[0], 16)
                act.sem_inc(spread_stored[1], 16)

                def high(chunk, s):
                    act.wait_ge(u_turned, chunk + 2)
                    act.wait_ge(pre_done, 2 * chunk)
                    A(uhi[:, s % 2], turned[:], ACT.Copy).then_inc(hi_done, 1)

                def spread_out(tile, g):
                    part, col = divmod(g, GROUPS // 2)
                    act.wait_ge(spread_done, tile * GROUPS + g + 1 + SLOTS)
                    if col == 0:
                        act.wait_ge(spread_stored[part], 16 * tile + 16)
                    A(spread[:, part, :, col * GROUP:(col + 1) * GROUP].rearrange("p e t -> p t e"),
                      spread_ps[:, g % 2], ACT.Copy).then_inc(spread_read, 1)
                    if col == GROUPS // 2 - 1:
                        act.wait_ge(spread_read, tile * GROUPS + g + 3)
                        act.dma_start(d.gates[bass.ds(2 * tile + part, 1)].rearrange("a p e t -> p (a e t)"),
                                      spread[:, part].rearrange("p e t -> p (e t)")).then_inc(spread_stored[part], 16)

                high(0, 0)

                def body(c0, tile, select):
                    turns, steps = slot_turns(c0, tile), steps_of(tile)
                    for s in range(steps):
                        if s + 1 < steps or select is not None:
                            high(c0 + s + 1, s + 1)
                        for half in range(2):
                            act.wait_ge(pre_done, 2 * (c0 + s) + half + 3)
                            if half == 0:
                                act.wait_ge(act_stored[s % 2], 16 * (turns + s // 2))
                            A(act_out[:, s % 2, half * HALF:(half + 1) * HALF], pre[:, half], ACT.Gelu_apprx_tanh
                              ).then_inc(act_done, 1)
                            if tile is not None:
                                for g in spread_at(s, half):
                                    spread_out(tile, g)
                        act.wait_ge(act_done, 2 * (c0 + s) + 3)
                        act.dma_start(d.acts[bass.ds(c0 + s, 1)].rearrange("a p t -> p (a t)"), act_out[:, s % 2]
                                      ).then_inc(act_stored[s % 2], 16)
                        if s == 11 and select is not None:
                            act.wait_ge(shifted, select + 1)
                            A(route[:, 2], route[:, 2], ACT.Exp).then_inc(exp_done, 1)
                passes(act, body)
                for b in range(2):
                    act.wait_ge(act_stored[b], 16 * (NK // 2))
                    act.wait_ge(spread_stored[b], 16 * NT + 16)

            @block.gpsimd
            def _(pool):
                def body(c0, tile, select):
                    if tile is None:
                        return
                    for g in range(GROUPS):
                        if g == 0:
                            pool.wait_ge(routeT_done, 3 * tile + 3)
                        pool.wait_ge(hot_done, tile * GROUPS + g + 1)
                        tokens = slice(g * GROUP, (g + 1) * GROUP)
                        pool.tensor_tensor(second_lo[:, g % SLOTS], second_hi[:, g % SLOTS].bitcast(F32),
                                           each(gate_lo[:, tokens]), ALU.mult)
                        pool.tensor_tensor(second_hi[:, g % SLOTS], second_hi[:, g % SLOTS].bitcast(F32),
                                           each(gate_hi[:, tokens].bitcast(F32)), ALU.mult).then_inc(gates_hot, 1)
                passes(pool, body)

            @block.vector
            def _(dve):
                v = nc.vector
                own = Done(dve, picked)
                iota = m.iota[:, 0:TOP]

                def low(chunk, s):
                    dve.wait_ge(hi_done, chunk + 1)
                    v.tensor_tensor(ulo[:, s % 2], turned[:], uhi[:, s % 2].bitcast(F32), ALU.subtract
                                    ).then_inc(lo_done, 1)

                def hot_group(tile, g):
                    dve.wait_ge(spread_done, tile * GROUPS + g + 1)
                    tokens = slice(g * GROUP, (g + 1) * GROUP)
                    v.tensor_tensor(first_hot[:, g % SLOTS], keys, each(routeT[:, 0, tokens]), ALU.is_equal)
                    v.tensor_tensor(second_hi[:, g % SLOTS], keys, each(routeT[:, 1, tokens]), ALU.is_equal
                                    ).then_inc(hot_done, 1)

                apart = sem("select_waits")

                def top(values, indices, source, left):
                    own.link_apart(v.max(values[:, 0:8], source), apart)
                    own.mark(v.max_index(indices[:, 0:8], values[:, 0:8], source))
                    own.link_apart(v.match_replace(left, values[:, 0:8], source, LOWEST), apart)
                    own.link_apart(v.max(values[:, 8:16], left), apart)
                    own.link_apart(v.max_index(indices[:, 8:16], values[:, 8:16], left), apart)

                def select_head(h):
                    for p in range(2):
                        top(val[:, h, p], idx[:, h, p], sc[:, 2 * h + p, :], rest[:, p])
                    own.link(v.tensor_tensor(cand[:], val[:, h, 0].rearrange("p (a b) -> p a b", b=1)
                                             .to_broadcast([P, TOP, TOP]),
                                             val[:, h, 1].rearrange("p (a b) -> p a b", a=1)
                                             .to_broadcast([P, TOP, TOP]), ALU.add))
                    dve.sem_inc(apart, 1)
                    top(pval[:, h], pidx[:, h], cand[:].rearrange("p a b -> p (a b)"), crest[:])

                def digits():
                    own.mark(v.tensor_scalar(pdig[:, 0], pidx[:], TOP.bit_length() - 1, None, ALU.logical_shift_right))
                    own.mark(v.tensor_scalar(pdig[:, 1], pidx[:], TOP - 1, None, ALU.bitwise_and))
                    own.link(v.tensor_copy(idxf[:], idx[:]))
                    own.link(v.tensor_copy(pdigf[:], pdig[:]))

                def key(p):
                    flat = pdigf[:, p].rearrange("p h (k a) -> p (h k) a", a=1)
                    own.link(v.tensor_tensor(hot, flat.to_broadcast([P, PH * TOP, TOP]),
                                             iota.rearrange("p (a b) -> p a b", a=1)
                                             .to_broadcast([P, PH * TOP, TOP]), ALU.is_equal))
                    own.link(v.tensor_tensor(hot.rearrange("p (h k) r -> p h k r", h=PH),
                                             hot.rearrange("p (h k) r -> p h k r", h=PH),
                                             idxf[:, :, p].rearrange("p h (a r) -> p h a r", a=1)
                                             .to_broadcast([P, PH, TOP, TOP]), ALU.mult))
                    own.link(v.tensor_reduce(route[:, p].rearrange("p h k -> p (h k)"), hot, AX_X, ALU.add))

                def body(c0, tile, select):
                    steps = steps_of(tile)
                    if tile is not None:
                        dve.wait_ge(route_turned, tile + 1)
                        dve.wait_ge(spread_done, tile * GROUPS + SLOTS)
                        v.tensor_copy(routeT[:], route_ps[:]).then_inc(routeT_done, 1)
                        dve.wait_ge(routeT_done, 3 * tile + 1)
                        v.tensor_copy(gate_hi[:], routeT[:, 2]).then_inc(routeT_done, 1)
                        dve.wait_ge(routeT_done, 3 * tile + 2)
                        v.tensor_tensor(gate_lo[:], routeT[:, 2], gate_hi[:].bitcast(F32), ALU.subtract
                                        ).then_inc(routeT_done, 1)
                        dve.wait_ge(routeT_done, 3 * tile + 3)
                    if select is not None:
                        own.enter(select, TILE_STEPS)
                    for s in range(steps):
                        if s + 1 < steps or select is not None:
                            low(c0 + s + 1, s + 1)
                        if tile is not None:
                            for g in groups_of(s):
                                hot_group(tile, g)
                        if select is None:
                            continue
                        if s == 1:
                            dve.wait_ge(sc_in, 16 * (select + 1))
                            dve.sem_inc(apart, 1)
                        if 1 <= s <= PH:
                            select_head(s - 1)
                        if s == 9:
                            digits()
                            if tile is not None:
                                dve.wait_ge(route_turned, select)
                            key(0)
                        if s == 10:
                            key(1)
                            dve.sem_inc(sc_used, 1)
                            v.tensor_tensor(route[:, 2], pval[:], pval[:, :, 0:1].to_broadcast([P, PH, TOP]), ALU.subtract
                                            ).then_inc(shifted, 1)
                        if s == 12:
                            dve.wait_ge(exp_done, select + 1)
                            own.link(v.tensor_reduce(gsum[:], route[:, 2], AX_X, ALU.add))
                            own.link(v.reciprocal(gsum[:], gsum[:]))
                            v.tensor_tensor(route[:, 2], route[:, 2],
                                            gsum[:].rearrange("p (h a) -> p h a", a=1).to_broadcast([P, PH, TOP]),
                                            ALU.mult).then_inc(route_done, 1)
                            assert own.count == TILE_STEPS, own.count

                dve.wait_ge(hi_done, 1)
                low(0, 0)
                passes(dve, body)


def experts_down(nc, d, m, sem):
    D, S, NK = d.D, d.S, d.NK
    NT = S // P
    C = 2
    BANKS = NT * D // HALF
    RING = 8
    v_rows = d.peer_v.rearrange("(p e) n -> p e n", p=NK)
    PASSES = NK // C // 2
    with ExitStack() as own_memory:
        sb = lambda n, s, t=F32: own_memory.enter_context(nc.sbuf_tensor(n, s, t))
        prod = sb("acts_times_gates", [P, 2, C, S])
        gate = sb("gates_group", [P, 2, 2 * NT, C, P // 2])
        vt = sb("v_group", [P, 2, C, D])
        whi, wlo = sb("w_hi", [P, 2, C, S], F32R), sb("w_lo", [P, 2, C, S], F32R)
        vhi, vlo = sb("v_hi", [P, 2, C, D], F32R), sb("v_lo", [P, 2, C, D], F32R)
        out = own_memory.enter_context(nc.psum_tensor("expert_out", [P, RING, HALF], F32))

        y_in = sem("x2_in")
        a_in, g_in, v_in = ([sem(f"{n}_in{b}") for b in range(2)] for n in ("acts", "gates", "v"))
        prod_done, whi_done, wlo_done = sem("prod_done"), sem("w_hi_done"), sem("w_lo_done")
        vhi_done, vlo_done = sem("v_hi_done"), sem("v_lo_done")
        out_done, out_read = sem("expert_out_done"), sem("expert_out_read")

        with nc.Block() as block:
            @block.sync
            def _(sp):
                with sp.Fori(0, PASSES) as i:
                    for b in range(2):
                        n = 2 * i + b
                        sp.wait_ge(vlo_done, C * n + 1)
                        sp.dma_start(vt[:, b], v_rows[:, bass.ds(C * n, C), :]).then_inc(v_in[b], 16)
                        sp.wait_ge(wlo_done, C * n + 1)
                        sp.dma_start(prod[:, b], d.acts[bass.ds(C * n, C)].rearrange("c p t -> p c t")
                                     ).then_inc(a_in[b], 16)
                        sp.dma_start(gate[:, b], d.gates[:, :, bass.ds(C * n, C), :].rearrange("t p c k -> p t c k")
                                     ).then_inc(g_in[b], 16)

            @block.gpsimd
            def _(pool):
                pool.sem_inc(vlo_done, C + 1)
                with pool.Fori(0, PASSES) as i:
                    for b in range(2):
                        for c in range(C):
                            pool.wait_ge(vhi_done, (2 * i + b) * C + c + 1)
                            pool.tensor_tensor(vlo[:, b, c], vt[:, b, c], vhi[:, b, c].bitcast(F32), ALU.subtract
                                               ).then_inc(vlo_done, 1)

            @block.scalar
            def _(act):
                act.dma_start(m.y[:], d.x2.rearrange("(t p) n -> p t n", p=P)).then_inc(y_in, 16)
                with act.Fori(0, PASSES) as i:
                    for b in range(2):
                        n = 2 * i + b
                        act.wait_ge(out_done, BANKS * n + 1)
                        act.wait_ge(v_in[b], 16 * (i + 1))
                        for c in range(C):
                            nc.scalar.activation(vhi[:, b, c], vt[:, b, c], ACT.Copy).then_inc(vhi_done, 1)
                        for c in range(C):
                            act.wait_ge(prod_done, C * n + c + 1)
                            nc.scalar.activation(whi[:, b, c], prod[:, b, c], ACT.Copy).then_inc(whi_done, 1)

            @block.vector
            def _(dve):
                v = nc.vector
                dve.sem_inc(wlo_done, C + 1)
                dve.sem_inc(out_read, RING)

                def multiply(i, b):
                    dve.wait_ge(a_in[b], 16 * (i + 1))
                    dve.wait_ge(g_in[b], 16 * (i + 1))
                    for c in range(C):
                        tokens = prod[:, b, c].rearrange("p (t k) -> p t k", k=P // 2)
                        v.tensor_tensor(tokens, tokens, gate[:, b, :, c, :], ALU.mult).then_inc(prod_done, 1)

                def low(n, b, c):
                    dve.wait_ge(whi_done, C * n + c + 1)
                    v.tensor_tensor(wlo[:, b, c], prod[:, b, c], whi[:, b, c].bitcast(F32), ALU.subtract
                                    ).then_inc(wlo_done, 1)

                def add(n, j):
                    t, half = divmod(j, 2)
                    dve.wait_ge(out_done, BANKS * n + j + 2 + BANKS)
                    cols = slice(half * HALF, (half + 1) * HALF)
                    v.tensor_tensor(m.y[:, t, cols], m.y[:, t, cols], out[:, j % RING], ALU.add).then_inc(out_read, 1)

                def prepare_beside_adds(i, b):
                    n = 2 * i + b
                    multiply(i, b)
                    for j in range(BANKS):
                        if j in (2, 4):
                            low(n, b, j // 2 - 1)
                        add(n - 1, j)

                multiply(0, 0)
                for c in range(C):
                    low(0, 0, c)
                dve.wait_ge(y_in, 16)
                prepare_beside_adds(0, 1)
                with dve.Fori(1, PASSES) as i:
                    for b in range(2):
                        prepare_beside_adds(i, b)
                for j in range(BANKS):
                    add(NK // C - 1, j)

            @block.tensor
            def _(pe):
                pe.sem_inc(out_done, BANKS + 1)
                with pe.Fori(0, PASSES) as i:
                    for b in range(2):
                        n = 2 * i + b
                        pe.wait_ge(wlo_done, C * n + 2 * C + 1)
                        pe.wait_ge(vlo_done, C * n + 2 * C + 1)
                        for j in range(BANKS):
                            t, half = divmod(j, 2)
                            rows, cols = slice(t * P, (t + 1) * P), slice(half * HALF, (half + 1) * HALF)
                            pe.wait_ge(out_read, BANKS * n + j + 1)
                            terms = [(a, e, c) for c in range(C) for a, e in ((whi, vhi), (whi, vlo), (wlo, vhi))]
                            for k, (a, e, c) in enumerate(terms):
                                last = nc.tensor.matmul(out[:, j % RING], a[:, b, c, rows], e[:, b, c, cols],
                                                        start=k == 0, stop=k == len(terms) - 1)
                            last.then_inc(out_done, 1)


def last_norm(nc, d, m, sem):
    D, NT = d.D, d.S // P
    with ExitStack() as own_memory:
        sb = lambda n, s, t=F32: own_memory.enter_context(nc.sbuf_tensor(n, s, t))
        gain, squares = sb("gain_last", [P, D]), sb("squares8", [P, 2, D])
        sums = sb("sums8", [P, NT])
        rows = sb("normed_rows", [P, NT, D])
        gain_in, summed, dve8, rooted = sem("gain8_in"), sem("y_summed"), sem("dve8"), sem("y_rooted")
        stored = [sem(f"out_stored{b}") for b in range(NT)]

        with nc.Block() as block:
            @block.sync
            def _(sp):
                sp.dma_start(gain[:], d.final_g.partition_broadcast(P)).then_inc(gain_in, 16)
                for b in range(NT):
                    sp.wait_ge(dve8, 2 + b + 1)
                    sp.dma_start(d.out[b * P:(b + 1) * P, :], rows[:, b, :]).then_inc(stored[b], 16)
                for b in range(NT):
                    sp.wait_ge(stored[b], 16)

            @block.scalar
            def _(act):
                for b in range(NT):
                    if b >= 2:
                        act.wait_ge(summed, b - 1)
                    nc.scalar.activation(squares[:, b % 2], m.y[:, b, :], ACT.Square, accum_out=sums[:, b:b + 1]
                                         ).then_inc(summed, 1)
                act.wait_ge(dve8, 1)
                nc.scalar.activation(sums[:], sums[:], ACT.Sqrt).then_inc(rooted, 1)

            @block.vector
            def _(dve):
                v = nc.vector
                own = Done(dve, dve8)
                dve.wait_ge(summed, NT)
                own.link(v.tensor_scalar(sums[:], sums[:], 1.0 / D, EPS, ALU.mult, ALU.add))
                dve.wait_ge(rooted, 1)
                own.link(v.reciprocal(sums[:], sums[:]))
                dve.wait_ge(gain_in, 16)
                for b in range(NT):
                    own.mark(v.scalar_tensor_tensor(out=rows[:, b, :], in0=m.y[:, b, :], scalar=sums[:, b:b + 1],
                                                    in1=gain[:], op0=ALU.mult, op1=ALU.mult))


def hybrid_block(nc, args, stop=None):
    d = Parts()
    d.x, d.norm1_g, d.w_in, d.conv_w = (args["x"], args["norm1_g"], args["w_in"], args["conv_w"])
    d.conv_b, d.lru_wa, d.lru_ba, d.lru_wx = (args["conv_b"], args["lru_wa"], args["lru_ba"], args["lru_wx"])
    d.lru_bx, d.lru_lambda, d.fox_bf, d.gn_lru_g = (args["lru_bx"], args["lru_lambda"], args["fox_bf"], args["gn_lru_g"])
    d.gn_fox_g, d.w_out, d.norm2_g, d.peer_wq = (args["gn_fox_g"], args["w_out"], args["norm2_g"], args["peer_wq"])
    d.peer_subkeys, d.peer_u, d.peer_v, d.final_g = (args["peer_subkeys"], args["peer_u"], args["peer_v"], args["final_g"])
    d.out = args["out"]
    d.S, d.D = d.x.shape
    d.GROUP, d.TAPS, d.FH = d.D // 2, d.conv_w.shape[0], d.fox_bf.shape[0]
    d.PAD = d.TAPS - 1
    d.LHD, d.FHD = d.lru_wa.shape[1], d.GROUP // d.FH
    d.QSCALE = float(d.FHD) ** -0.5
    d.PH, d.NK, d.TOP = d.peer_subkeys.shape[0] // 2, d.peer_subkeys.shape[1], 16
    NT, CT, KT = d.S // P, d.GROUP // P, d.D // P
    scratch = lambda n, s: nc.dram_tensor(n, s, F32, kind="Internal").ap()
    d.x2 = scratch("x2_dram", [d.S, d.D])
    d.scores = scratch("scores_dram", [NT, P, 2 * d.PH, d.NK])
    d.acts = scratch("acts_dram", [d.NK, d.NK, d.S])
    d.gates = scratch("gates_dram", [2 * NT, d.NK, d.NK, P // 2])

    with ExitStack() as memory:
        def sem(name):
            return memory.enter_context(nc.semaphore(name))

        m = Parts()
        m.d = d
        sb = lambda stack, n, s, t=F32, **k: stack.enter_context(nc.sbuf_tensor(n, s, t, **k))
        m.ident = sb(memory, "ident", [P, P])
        m.iota = sb(memory, "iota", [P, P])
        m.ones_col = sb(memory, "ones_col", [P, 1])
        m.rstd_lru = sb(memory, "rstd_lru", [P, NT])

        m.ident_ready = sem("ident_ready")
        with nc.Block() as block:
            @block.gpsimd
            def _(pool):
                pool.memset(m.ident[:], 0.0).then_inc(m.ident_ready, 1)
                pool.wait_ge(m.ident_ready, 1)
                pool.affine_select(out=m.ident[:], in_=m.ident[:], compare_op=ALU.not_equal, fill=1.0, base=0,
                                   pattern=[[-1, P]], channel_multiplier=1).then_inc(m.ident_ready, 1)
                pool.iota(m.iota[:], [[1, P]], base=0, channel_multiplier=0, allow_small_or_imprecise_dtypes=True)
                pool.memset(m.ones_col[:], 1.0)

        with ExitStack() as groups:
            m.gateT = sb(groups, "gateT", [P, CT, d.S])
            conv_row = d.PAD + d.S
            shared = sb(groups, "x_proj_then_attention", [P, CT * conv_row])
            m.xrT = shared[:].rearrange("p (c s) -> p c s", s=conv_row)
            m.fox = shared[:, 0:NT * d.GROUP].rearrange("p (t n) -> p t n", n=d.GROUP)
            with ExitStack() as heads:
                m.qk = sb(heads, "qT_kT", [P, 2, CT, d.S])
                m.qT, m.kT = m.qk[:, 0], m.qk[:, 1]
                m.v = sb(heads, "v_heads", [P, NT, d.GROUP])
                m.forget = sb(heads, "forget", [d.FH, d.S])
                with ExitStack() as early:
                    m.hT = sb(early, "hT", [P, KT, d.S])
                    m.w_qkv = sb(early, "w_qkv", [P, 2, KT, d.GROUP // 2])
                    m.w_qkv_in = [sem("w_qkv_in0"), sem("w_qkv_in1")]
                    m.wa, m.wx = sb(early, "wa_blocks", [P, CT, P]), sb(early, "wx_blocks", [P, CT, P])
                    m.taps = sb(early, "conv_taps", [P, CT, d.TAPS])
                    m.lru_vec = sb(early, "lru_vectors", [P, 5, CT])
                    project(nc, d, m, sem)
                    recur(nc, d, m, sem)
                if stop == "recur": return m
                attend(nc, d, m, sem)
                if stop == "attend": return m
            h2 = ExitStack()
            m.h2T = sb(h2, "h2T", [P, 2, KT, d.S], F32R, side="right")
            mix_out(nc, d, m, sem)
        if stop == "mix": return m
        with h2:
            score(nc, d, m, sem)
            if stop == "score": return m
            experts_up(nc, d, m, sem)
        if stop == "up": return m
        m.y = sb(memory, "y", [P, NT, d.D])
        experts_down(nc, d, m, sem)
        last_norm(nc, d, m, sem)


_INS = ["x", "norm1_g", "w_in", "conv_w", "conv_b", "lru_wa", "lru_ba", "lru_wx", "lru_bx", "lru_lambda", "fox_bf",
        "gn_lru_g", "gn_fox_g", "w_out", "norm2_g", "peer_wq", "peer_subkeys", "peer_u", "peer_v", "final_g"]


def kernel(**inputs):
    import numpy as _np
    import concourse.bacc as _bacc
    from concourse.bass_utils import run_bass_kernel_spmd as _run

    nc = _bacc.Bacc("TRN2", target_bir_lowering=False, num_devices=1)
    arrays, args = {}, {}
    for name in _INS:
        a = _np.ascontiguousarray(inputs[name])
        if name != "final_g":
            a = a.reshape(a.shape[1:])
        if name == "peer_subkeys":
            a = a.reshape((-1,) + a.shape[2:])
        arrays[f"in_{name}"] = a
        args[name] = nc.dram_tensor(f"in_{name}", a.shape, mybir.dt.from_np(a.dtype), kind="ExternalInput").ap()
    shape = inputs["x"].shape
    args["out"] = nc.dram_tensor("out_rows", shape[1:], F32, kind="ExternalOutput").ap()
    hybrid_block(nc, args)
    r = _run(nc, [arrays], core_ids=[0])
    return r.results[0]["out_rows"].reshape(shape)
```
